# Optimizing a Trainium2 kernel written in Bass

```python
import jax, jax.numpy as jnp
from jax import lax
import numpy as np

D_MODEL = 1024
BATCH = 1
SEQ = 1024
DEPTH = 2
DEC_BATCH = 1
DEC_SEQ = 32
PAST_LEN = 2048

CHUNK = 64
N_MIXERS = 2
N_A = (DEPTH + 1) // 2
N_B = DEPTH // 2
CONV_W = 3
CONV_HIST = CONV_W - 1
POOL_WINDOWS = (2, 4, 8, 16)
N_POOL_GROUPS = len(POOL_WINDOWS)
POOL_GROUP = D_MODEL // N_POOL_GROUPS
POOL_HIST = max(POOL_WINDOWS) - 1
D_FF = 4 * D_MODEL
D_PLE = 256
ALPHA = (2 * DEPTH) ** 0.25
BETA = (8 * DEPTH) ** -0.25
LN_EPS = 1e-5

kernel_name = "hybrid_shortconv_pool_streaming_step"

def layer_norm(x, g, b):
    xf = x.astype(jnp.float32)
    mu = jnp.mean(xf, axis=-1, keepdims=True)
    xc = xf - mu
    var = jnp.mean(xc * xc, axis=-1, keepdims=True)
    return (xc * lax.rsqrt(var + LN_EPS) * g.astype(jnp.float32) + b.astype(jnp.float32)).astype(x.dtype)

def short_conv_mixer(x, hist, w_in, conv_w, w_out):
    s = x.shape[1]
    gb, gc, h = jnp.split(x @ w_in, 3, axis=-1)
    u = gc * h
    ext = jnp.concatenate([hist.astype(u.dtype), u], axis=1)
    conv = ext[:, 0:s] * conv_w[0] + ext[:, 1:1 + s] * conv_w[1] + ext[:, 2:2 + s] * conv_w[2]
    y = (gb * conv) @ w_out
    return y, ext[:, -CONV_HIST:]

def pool_mixer(x, hist, pos0, w_grp, scale):
    b, s, _ = x.shape
    ext = jnp.concatenate([hist.astype(x.dtype), x], axis=1)
    cs = jnp.cumsum(ext.astype(jnp.float32), axis=1)
    cs = jnp.concatenate([jnp.zeros((b, 1, D_MODEL), jnp.float32), cs], axis=1)
    pos = pos0 + jnp.arange(s)
    means = []
    for g, w in enumerate(POOL_WINDOWS):
        lo, hi = g * POOL_GROUP, (g + 1) * POOL_GROUP
        win = cs[:, POOL_HIST + 1:POOL_HIST + 1 + s, lo:hi] - cs[:, POOL_HIST + 1 - w:POOL_HIST + 1 - w + s, lo:hi]
        cnt = jnp.minimum(pos + 1, w).astype(jnp.float32)[None, :, None]
        means.append(win / cnt)
    d = (jnp.concatenate(means, axis=-1) - x.astype(jnp.float32)).astype(x.dtype)
    d = d.reshape(b, s, N_POOL_GROUPS, POOL_GROUP)
    y = jnp.einsum('bsgc,gcd->bsgd', d, w_grp).reshape(b, s, D_MODEL) * scale
    return y, ext[:, -POOL_HIST:]

def stack_or_empty(rows, b, t, dtype):
    if rows:
        return jnp.stack(rows, axis=0)
    return jnp.zeros((0, b, t, D_MODEL), dtype)

def trunk(x, p, conv_states, pool_states, pos0, a_w_in, a_conv_w, a_w_out, b_w_grp, b_scale,
          ln1_g, ln1_b, ln2_g, ln2_b, mlp_w1, mlp_w2, ple_w, ple_gate_w):
    bsz = x.shape[0]
    new_conv, new_pool = [], []
    for i in range(DEPTH):
        j = i // N_MIXERS
        if i % N_MIXERS == 0:
            y, nh = short_conv_mixer(x, conv_states[j], a_w_in[j], a_conv_w[j], a_w_out[j])
            new_conv.append(nh)
        else:
            y, nh = pool_mixer(x, pool_states[j], pos0, b_w_grp[j], b_scale[j])
            new_pool.append(nh)
        h = layer_norm(ALPHA * x + y, ln1_g[i], ln1_b[i])
        r = jax.nn.relu(h @ mlp_w1[i])
        f = (r * r) @ mlp_w2[i]
        e = (p[i] @ ple_w[i]) * jax.nn.sigmoid(h @ ple_gate_w[i])
        x = layer_norm(ALPHA * h + f + e, ln2_g[i], ln2_b[i])
    return (x, stack_or_empty(new_conv, bsz, CONV_HIST, x.dtype),
            stack_or_empty(new_pool, bsz, POOL_HIST, x.dtype))

def setup_inputs(seed: int = 0) -> dict:
    key = jax.random.key(seed)
    ks = jax.random.split(key, 20)
    f32 = jnp.float32
    n = lambda k, shape, s: jax.random.normal(k, shape, f32) * s
    return {
        "x_prompt": n(ks[0], (BATCH, SEQ, D_MODEL), 1.0),
        "x_sample": n(ks[1], (DEC_BATCH, DEC_SEQ, D_MODEL), 1.0),
        "state_conv": n(ks[2], (N_A, DEC_BATCH, CONV_HIST, D_MODEL), 1.0),
        "state_pool": n(ks[3], (N_B, DEC_BATCH, POOL_HIST, D_MODEL), 1.0),
        "p_prompt": n(ks[4], (DEPTH, BATCH, SEQ, D_PLE), 1.0),
        "p_sample": n(ks[5], (DEPTH, DEC_BATCH, DEC_SEQ, D_PLE), 1.0),
        "a_w_in": n(ks[6], (N_A, D_MODEL, 3 * D_MODEL), D_MODEL ** -0.5),
        "a_conv_w": n(ks[7], (N_A, CONV_W, D_MODEL), CONV_W ** -0.5),
        "a_w_out": n(ks[8], (N_A, D_MODEL, D_MODEL), BETA * D_MODEL ** -0.5),
        "b_w_grp": n(ks[9], (N_B, N_POOL_GROUPS, POOL_GROUP, POOL_GROUP), BETA * POOL_GROUP ** -0.5),
        "b_scale": 1.0 + n(ks[10], (N_B, D_MODEL), 0.1),
        "ln1_g": 1.0 + n(ks[11], (DEPTH, D_MODEL), 0.05),
        "ln1_b": n(ks[12], (DEPTH, D_MODEL), 0.02),
        "ln2_g": 1.0 + n(ks[13], (DEPTH, D_MODEL), 0.05),
        "ln2_b": n(ks[14], (DEPTH, D_MODEL), 0.02),
        "mlp_w1": n(ks[15], (DEPTH, D_MODEL, D_FF), D_MODEL ** -0.5),
        "mlp_w2": n(ks[16], (DEPTH, D_FF, D_MODEL), BETA * D_FF ** -0.5),
        "ple_w": n(ks[17], (DEPTH, D_PLE, D_MODEL), BETA * D_PLE ** -0.5),
        "ple_gate_w": n(ks[18], (DEPTH, D_MODEL, D_MODEL), D_MODEL ** -0.5),
    }

def reference(x_prompt, x_sample, state_conv, state_pool, p_prompt, p_sample,
              a_w_in, a_conv_w, a_w_out, b_w_grp, b_scale,
              ln1_g, ln1_b, ln2_g, ln2_b, mlp_w1, mlp_w2, ple_w, ple_gate_w):
    weights = (a_w_in, a_conv_w, a_w_out, b_w_grp, b_scale,
               ln1_g, ln1_b, ln2_g, ln2_b, mlp_w1, mlp_w2, ple_w, ple_gate_w)
    zero_conv = jnp.zeros((N_A, BATCH, CONV_HIST, D_MODEL), x_prompt.dtype)
    zero_pool = jnp.zeros((N_B, BATCH, POOL_HIST, D_MODEL), x_prompt.dtype)
    y_prompt, conv_prompt_new, pool_prompt_new = trunk(
        x_prompt, p_prompt, zero_conv, zero_pool, 0, *weights)
    y_sample, conv_sample_new, pool_sample_new = trunk(
        x_sample, p_sample, state_conv, state_pool, PAST_LEN, *weights)
    return (y_prompt, y_sample, conv_prompt_new, conv_sample_new, pool_prompt_new, pool_sample_new)


_drawn_inputs = setup_inputs


def setup_inputs(seed=0):
    import zlib

    import numpy as np

    out = dict(_drawn_inputs(seed))
    spreads = {}
    factors = {}
    for name, (base, spread) in spreads.items():
        noise = np.random.default_rng([zlib.crc32(name.encode()), seed]).standard_normal(out[name].shape)
        drawn = base * np.exp(spread * noise) if base else spread * noise
        out[name] = __import__('jax').numpy.asarray(drawn.astype(out[name].dtype))
    for name, factor in factors.items():
        out[name] = (out[name] * factor).astype(out[name].dtype)
    return out
```

```python
from contextlib import ExitStack

import concourse.bass as bass
from concourse import mybir

F32 = mybir.dt.float32
F32R = mybir.dt.float32r
ALU = mybir.AluOpType
ACT = mybir.ActivationFunctionType

P = 128
D = 1024
KD = D // P
PROMPT, SAMPLE = 1024, 32
TOKENS = PROMPT + SAMPLE
NG = 3
TG = TOKENS // NG
TAIL = PROMPT - (NG - 1) * TG
FF = 4 * D
CHUNK = 2
NCH = FF // P // CHUNK
PLE = 256
KP = PLE // P
WINDOWS = (2, 4, 8, 16)
HIST = 15
CH = 2
DEPTH = 2
ALPHA = (2 * DEPTH) ** 0.25
EPS = 1e-5
U = 1024
GCOLS = KD * TG


def weight_units():
    names = [("in", m, j) for m in range(KD) for j in range(3)]
    names += [("out", m) for m in range(KD)]
    for layer in range(DEPTH):
        if layer == 0:
            names += [("ple", 0, 0), ("ple", 0, 1)]
            names += [("gate", 0, m) for m in range(4)]
        else:
            names += [("grp", 0), ("grp", 1)]
            names += [("gate", 1, m) for m in range(4)]
            names += [("ple", 1, 0), ("ple", 1, 1)]
        names += [("p", layer, n) for n in range(NG)]
        names += [("gate", layer, m) for m in range(4, 8)]
        names += [("mlp", layer, c, j) for c in range(NCH) for j in range(4)]
    units, uses, q = {}, [0] * 4, 0
    for s, name in enumerate(names):
        if name[0] == "in" or name in (("out", 0), ("out", 1), ("out", 2)):
            q = s % 3
        units[name] = (s, q, uses[q])
        uses[q] += 1
        q = (q + 1) % 4
    return units


def bass_streaming_trunk(nc, x_t, w_stream, p_t, vectors, conv_hist, pool_hist, y_t, conv_new, pool_new):
    units = weight_units()
    order = sorted(units, key=lambda name: units[name][0])
    V_CONV, V_SCALE, V_LN, V_RATIO = 0, 3 * KD, 4 * KD, 4 * KD + 4 * 2 * KD
    NV = V_RATIO + len(WINDOWS) * HIST

    with ExitStack() as ctx:
        cursor = [-(-nc.sbuf_base // 32) * 32]

        def place(name, shape, dt, at=None):
            size = 4
            for n in shape[1:]:
                size *= n
            if at is None:
                at = cursor[0]
                cursor[0] += -(-size // 32) * 32
            return nc.alloc_sbuf_tensor_at(name, shape, dt, offset=at), at

        def sem(name):
            return ctx.enter_context(nc.semaphore(name))

        big = [P, NG * GCOLS]
        half = NG * GCOLS * 4
        xh, at1 = place("x_hi", big, F32R)
        acc, _ = place("acc", big, F32, at1)
        xl, at2 = place("x_lo", big, F32R)
        lnt, _ = place("ln_squares", [P, GCOLS], F32, at2)
        at3 = at2 + GCOLS * 4
        rh, _ = place("r_hi", [P, NG * CHUNK * TG], F32R, at3)
        rl, _ = place("r_lo", [P, NG * CHUNK * TG], F32R, at3 + NG * CHUNK * TG * 4)
        WIN = HIST + TG + HIST
        wa, _ = place("win_a", [P, 2, 2, WIN], F32, at3)
        wb, _ = place("win_b", [P, 2, 2, WIN], F32, at3 + -(-4 * 4 * WIN // 32) * 32)
        at4 = at3 + 2 * NG * CHUNK * TG * 4
        tt, _ = place("t", [P, 2, TG], F32, at4)
        sq, _ = place("sq", [P, 2, TG], F32, at4 + 2 * TG * 4)
        assert at4 + 4 * TG * 4 <= at2 + half
        hh, at5 = place("h_hi", big, F32R)
        hl, at6 = place("h_lo", big, F32R)
        xraw, _ = place("x_raw", big, F32, at6)
        ws, at7 = place("w_split", [P, 6, 2, U], F32R)
        at8 = at7 + 4 * 2 * U * 4
        UW = CH + PROMPT + CH + SAMPLE
        CW = TG + CH
        ub, _ = place("u", [P, UW], F32, at8)
        at9 = at8 + -(-UW * 4 // 32) * 32
        gcs, _ = place("gc", [P, NG, TG], F32, at9)
        cv, _ = place("conv", [P, NG, CW], F32, at9 + NG * TG * 4)
        assert at9 + (NG * TG + NG * CW) * 4 <= at8 + 2 * 2 * U * 4
        raw, _ = place("w_raw", [P, 4, U], F32)
        ones, _ = place("ones", [P, P], F32)
        vec, _ = place("vec", [P, NV], F32)
        chist, _ = place("conv_history", [P, KD * CH], F32)
        phist, _ = place("pool_history", [P, KD, HIST], F32)
        cnew, _ = place("conv_state", [P, KD * 2 * CH], F32)
        zeros, _ = place("zeros", [P, 2, HIST], F32)
        tails, _ = place("tails", [P, 2, KD, HIST], F32)
        s_mean, _ = place("sum_mean", [P, TG], F32)
        s_var, _ = place("sum_var", [P, TG], F32)
        std, _ = place("std", [P, TG], F32)
        var, _ = place("var", [P, TG], F32)
        rstd, _ = place("rstd", [P, TG], F32)
        assert cursor[0] <= nc.sbuf_usable_end, (cursor[0], nc.sbuf_usable_end)
        ps = ctx.enter_context(nc.psum_tensor("ps", [P, 8, 512], F32))
        VAR_BANK, MEAN_BANK, B_BANK = 2, 7, 3

        x_in = [sem(f"x_in{n}") for n in range(NG)]
        small_in = sem("small_in")
        raw_in = [sem(f"raw_in{q}") for q in range(4)]
        out_done = sem("out_done")
        state_out = sem("state_out")
        w_hi, w_lo = sem("w_hi"), sem("w_lo")
        x_hi_done, x_ready = sem("x_hi_done"), sem("x_ready")
        setup = sem("setup")
        act_passed, pool_passed = sem("act_passed"), sem("pool_passed")
        gc_full, h_full, gb_full = sem("gc_full"), sem("h_full"), sem("gb_full")
        gc_copied, u_done, tap0, tap1, tap2 = (sem(n) for n in ("gc_copied", "u_done", "tap0", "tap1", "tap2"))
        zf_done, z_hi_done, z_ready = sem("zf_done"), sem("z_hi_done"), sem("z_ready")
        hist_in, u_saved = sem("hist_in"), sem("u_saved")
        a_full, a_free, b_full, b_free = sem("a_full"), sem("a_free"), sem("b_full"), sem("b_free")
        out_free, out_added = sem("out_free"), sem("out_added")
        gate_added = sem("gate_added")
        sq_done, r_hi_done, r_ready = sem("sq_done"), sem("r_hi_done"), sem("r_ready")
        win_in, win_done, d_done, d_hi_done, d_ready = (sem(n) for n in ("win_in", "win_done", "d_done", "d_hi_done", "d_ready"))
        win_step, d_step = sem("win_step"), sem("d_step")
        y_scaled, y_added, tail_saved = sem("y_scaled"), sem("y_added"), sem("tail_saved")
        mean_sum, var_sum, mean_full, var_full = (sem(n) for n in ("mean_sum", "var_sum", "mean_full", "var_full"))
        centred, squared, std_done, var_copied, normed, affine, ln_hi, h_ready, ln_step = (
            sem(n) for n in ("centred", "squared", "std_done", "var_copied", "normed", "affine", "ln_hi", "h_ready", "ln_step"))

        block = ctx.enter_context(nc.Block())

        def wait(eng, s, value):
            if not isinstance(value, int) or value > 0:
                eng.wait_ge(s, value)

        def blk(t, n, k):
            at = n * GCOLS + k * TG
            return t[:, at:at + TG] if isinstance(at, int) else t[:, bass.ds(at, TG)]

        def grp(t, n):
            return t[:, n * GCOLS:(n + 1) * GCOLS]

        def grp3(t, n):
            return grp(t, n).rearrange("p (k t) -> p k t", k=KD)

        def f32(ap):
            return ap.bitcast(F32)

        def rpart(t, n, f):
            at = (n * CHUNK + f) * TG
            return t[:, at:at + TG]

        def lnv(stage, which, k):
            at = V_LN + (stage * 2 + which) * KD + k
            return vec[:, at:at + 1]

        def pieces(n):
            return ((0, TG, HIST),) if n < NG - 1 else ((0, TAIL, HIST), (TAIL, TG, 2 * HIST))

        def sums(w):
            return (wb if w % 2 == 0 else wa)[:, w % 2]

        A_GATE = [0, 24 + 6 * NCH]
        A_MLP = [a + 24 for a in A_GATE]
        OUT_TILES = 24
        B_GATE = [0, 24 + 24 * NCH + 24]
        B_MLP = [b + 24 for b in B_GATE]
        B_GRP = B_MLP[0] + 24 * NCH
        BF_GATE = [0, 24 + 24 * NCH]

        @block.sync
        def _(sp):
            def load(name):
                s, q, use = units[name]
                if use > 0:
                    before = max(units[o][0] for o in order[:s] if units[o][1] == q)
                    sp.wait_ge(w_lo, before + 1)
                if name[0] == "p":
                    src = p_t[(name[1] * NG + name[2]) * P:(name[1] * NG + name[2] + 1) * P, :]
                    sp.dma_start(raw[:, q, 0:KP * TG], src).then_inc(raw_in[q], 16)
                else:
                    row = stream_row[name] * P
                    sp.dma_start(raw[:, q, :], w_stream[row:row + P, :]).then_inc(raw_in[q], 16)

            stream_row = {}
            for name in order:
                if name[0] != "p":
                    stream_row[name] = len(stream_row)

            sp.dma_start(grp(xraw, 0), x_t[:, 0:GCOLS]).then_inc(x_in[0], 16)
            for j in range(3):
                load(("in", 0, j))
            sp.dma_start(vec[:], vectors).then_inc(small_in, 16)
            sp.dma_start(chist[:], conv_hist).then_inc(small_in, 16)
            sp.dma_start(phist[:], pool_hist.rearrange("p (k t) -> p k t", k=KD)).then_inc(small_in, 16)
            for n in range(1, NG):
                sp.dma_start(grp(xraw, n), x_t[:, n * GCOLS:(n + 1) * GCOLS]).then_inc(x_in[n], 16)
            with sp.Fori(1, KD + 1) as m:
                for j in range(3):
                    sp.wait_ge(w_lo, m * 3 + (j - 2))
                    sp.dma_start(raw[:, j, :], w_stream[bass.ds((m * 3 + j) * P, P), :]).then_inc(raw_in[j], 16)

            def load_from(first, last):
                for name in order[units[first][0]:units[last][0] + 1]:
                    load(name)

            def load_mlp(layer):
                load_from(("mlp", layer, 0, 0), ("mlp", layer, 0, 3))
                s0, row0 = units["mlp", layer, 0, 0][0], stream_row["mlp", layer, 0, 0]
                with sp.Fori(1, NCH) as c:
                    for j in range(4):
                        q = units["mlp", layer, 0, j][1]
                        sp.wait_ge(w_lo, c * 4 + (s0 + j - 3))
                        sp.dma_start(raw[:, q, :], w_stream[bass.ds((c * 4 + (row0 + j)) * P, P), :]).then_inc(raw_in[q], 16)

            load_from(("out", 3), ("gate", 0, 7))
            load_mlp(0)
            load_from(("grp", 0), ("gate", 1, 3))
            sp.wait_ge(affine, 2 * NG)
            a2 = grp3(acc, NG - 1)
            sp.dma_start(pool_new[:, :, 0:HIST], a2[:, :, TAIL - HIST:TAIL]).then_inc(state_out, 16)
            sp.dma_start(pool_new[:, :, HIST:2 * HIST], a2[:, :, TG - HIST:TG]).then_inc(state_out, 16)
            load_from(("ple", 1, 0), ("gate", 1, 7))
            load_mlp(1)
            sp.wait_ge(u_saved, KD)
            sp.dma_start(conv_new, cnew[:]).then_inc(out_done, 16)
            for n in range(NG):
                sp.wait_ge(affine, 3 * NG + n + 1)
                sp.dma_start(y_t[:, n * GCOLS:(n + 1) * GCOLS], grp(acc, n)).then_inc(out_done, 16)
            sp.wait_ge(out_done, 16 * (NG + 1))
            sp.wait_ge(state_out, 32)

        @block.tensor
        def _(pe):
            def triple(out, slot, col, mov_h, mov_l, first, last):
                wh, wl = ws[:, slot, 0, col:col + P], ws[:, slot, 1, col:col + P]
                pe.matmul(out, wh, mov_h, start=first, stop=False)
                pe.matmul(out, wh, mov_l, start=False, stop=False)
                return pe.matmul(out, wl, mov_h, start=False, stop=last)

            def full_tile(out, slot, src_h, src_l, n):
                for k in range(KD):
                    mm = triple(out, slot, k * P, blk(src_h, n, k), blk(src_l, n, k), k == 0, k == KD - 1)
                return mm

            def split_ready(name):
                wait(pe, w_lo, units[name][0] + 1)

            def conv_in(m):
                for n in range(NG):
                    if isinstance(m, int):
                        pe.wait_ge(x_ready, n + 1)
                    for j, (full, freed) in enumerate(((gc_full, gc_copied), (h_full, u_done), (gb_full, zf_done))):
                        if n == 0:
                            wait(pe, w_lo, m * 3 + (j + 1))
                        wait(pe, freed, m * 3 + n)
                        full_tile(ps[:, j, 0:TG], j, xh, xl, n).then_inc(full, 1)

            def mean(i):
                pe.wait_ge(mean_sum, i + 1)
                wait(pe, centred, i)
                pe.matmul(ps[:, MEAN_BANK, 0:TG], ones[:], s_mean[:], start=True, stop=True).then_inc(mean_full, 1)

            def variance(i):
                pe.wait_ge(var_sum, i + 1)
                wait(pe, var_copied, i)
                pe.matmul(ps[:, VAR_BANK, 0:TG], ones[:], s_var[:], start=True, stop=True).then_inc(var_full, 1)

            def conv_out(half, n, mm):
                i = (half * NG + n) * 4 + mm
                if n == 0:
                    split_ready(("out", 4 * half + mm))
                wait(pe, out_free, i - 1)
                full_tile(ps[:, i % 2, 0:TG], mm, hh, hl, n).then_inc(a_full, 1)

            def ple(layer, half, i):
                n, mm = i // 4, i % 4
                b = half * 12 + i
                wait(pe, b_free, BF_GATE[layer] + b - 3)
                out = ps[:, B_BANK + b % 4, 0:TG]
                for k in range(KP):
                    last = triple(out, 4 + k, (4 * half + mm) * P, rpart(rh, n, k), rpart(rl, n, k), k == 0, k == KP - 1)
                last.then_inc(b_full, 1)

            def gate(layer, half, i):
                n, mm = i // 4, i % 4
                a = half * 12 + i
                if n == 0:
                    split_ready(("gate", layer, 4 * half + mm))
                wait(pe, a_free, A_GATE[layer] + a - 1)
                full_tile(ps[:, a % 2, 0:TG], mm, hh, hl, n).then_inc(a_full, 1)

            def gates(layer):
                if layer == 0:
                    pe.wait_ge(out_free, OUT_TILES)
                else:
                    pe.wait_ge(y_scaled, 24)
                split_ready(("ple", layer, 1))
                split_ready(("p", layer, NG - 1))
                for half in range(2):
                    for i in range(3):
                        ple(layer, half, i)
                    for i in range(12):
                        if half == 0 and i % 4 == 0:
                            pe.wait_ge(h_ready, NG * layer + i // 4 + 1)
                        gate(layer, half, i)
                        if i + 3 < 12:
                            ple(layer, half, i + 3)

            def up(layer, c, n):
                for mm in range(CHUNK):
                    a = A_MLP[layer] + n * CHUNK + mm
                    if n == 0:
                        pe.wait_ge(w_lo, c * 4 + (units["mlp", layer, 0, mm][0] + 1))
                    pe.wait_ge(a_free, c * (NG * CHUNK) + (a - 1))
                    full_tile(ps[:, a % 2, 0:TG], mm, hh, hl, n).then_inc(a_full, 1)

            def down(layer, c, n, blocks=range(KD)):
                if 0 in blocks:
                    if n == 0:
                        pe.wait_ge(w_lo, c * 4 + (units["mlp", layer, 0, 3][0] + 1))
                    pe.wait_ge(r_ready, c * (NG * CHUNK) + (layer * NCH * NG * CHUNK + (n + 1) * CHUNK))
                for m in blocks:
                    b = n * KD + m
                    pe.wait_ge(b_free, c * (NG * KD) + (BF_GATE[layer] + 24 + b - 3))
                    out = ps[:, B_BANK + b % 4, 0:TG]
                    for f in range(CHUNK):
                        last = triple(out, 2 + f, m * P, rpart(rh, n, f), rpart(rl, n, f), f == 0, f == CHUNK - 1)
                    last.then_inc(b_full, 1)

            def mlp(layer):
                up(layer, 0, 0)
                with pe.Fori(0, NCH - 1) as c:
                    up(layer, c, 1)
                    down(layer, c, 0)
                    up(layer, c, 2)
                    down(layer, c, 1)
                    up(layer, c + 1, 0)
                    down(layer, c, 2)
                i = NG * (2 * layer + 1)
                c = NCH - 1
                up(layer, c, 1)
                down(layer, c, 0)
                up(layer, c, 2)
                mean(i)
                down(layer, c, 1)
                down(layer, c, 2, range(0, 4))
                variance(i)
                down(layer, c, 2, range(4, 8))
                if layer == 0:
                    split_ready(("grp", 1))
                    pe.wait_ge(b_free, BF_GATE[1])
                for n in range(1, NG):
                    mean(i + n)
                    variance(i + n)
                    if layer == 0:
                        for q in range(4):
                            grouped(n - 1, q)

            def grouped(n, q):
                pe.wait_ge(d_ready, n * 4 + q + 1)
                for m in (2 * q, 2 * q + 1):
                    b = n * KD + m
                    wait(pe, y_scaled, b - 3)
                    out = ps[:, B_BANK + b % 4, 0:TG]
                    for k in range(2):
                        col = ((q % 2) * 2 + k) * 256 + (m % 2) * P
                        last = triple(out, 4 + q // 2, col, blk(hh, n, 2 * q + k), blk(hl, n, 2 * q + k), k == 0, k == 1)
                    last.then_inc(b_full, 1)

            conv_in(0)
            with pe.Fori(1, KD) as m:
                conv_in(m)
            pe.wait_ge(z_ready, KD * NG)
            for half in range(2):
                for n in range(NG):
                    for mm in range(4):
                        conv_out(half, n, mm)
                        if half == 1:
                            if (n, mm) == (1, 1):
                                mean(0)
                            if (n, mm) == (2, 0):
                                variance(0)
                            if (n, mm) == (2, 2):
                                mean(1)
            variance(1)
            mean(2)
            variance(2)
            gates(0)
            mlp(0)
            for q in range(4):
                grouped(NG - 1, q)
            for i in range(6, 9):
                mean(i)
                variance(i)
            gates(1)
            mlp(1)

        @block.scalar
        def _(act):
            def split_hi(name, slot):
                s, q, use = units[name]
                act.wait_ge(raw_in[q], 16 * (use + 1))
                act.copy(ws[:, slot, 0, :], raw[:, q, :]).then_inc(w_hi, 1)

            def split_p(layer, n):
                s, q, use = units["p", layer, n]
                act.wait_ge(raw_in[q], 16 * (use + 1))
                act.copy(rh[:, n * KP * TG:(n + 1) * KP * TG], raw[:, q, 0:KP * TG]).then_inc(w_hi, 1)

            def split_x(n):
                act.wait_ge(x_in[n], 16)
                act.copy(grp(xh, n), grp(xraw, n)).then_inc(x_hi_done, 1)

            def conv_in(m):
                def split_next(j):
                    act.wait_ge(raw_in[j], m * 16 + 32)
                    act.copy(ws[:, j, 0, :], raw[:, j, :]).then_inc(w_hi, 1)

                for n in range(NG):
                    act.wait_ge(gc_full, m * 3 + (n + 1))
                    wait(act, z_ready, m * 3 + (n - 2))
                    act.copy(gcs[:, n, :], ps[:, 0, 0:TG]).then_inc(gc_copied, 1)
                    if n == NG - 1:
                        split_next(0)
                        act.wait_ge(hist_in, m + 1)
                    act.wait_ge(u_done, m * 3 + (n + 1))
                    act.sem_inc(act_passed, 1)
                    width = TG if n < NG - 1 else CW
                    w0 = vec[:, bass.ds(m * 3, 1)] if not isinstance(m, int) else vec[:, m * 3:m * 3 + 1]
                    act.mul(cv[:, n, 0:width], ub[:, n * TG:n * TG + width], w0).then_inc(tap0, 1)
                    if n == NG - 1:
                        split_next(1)
                    act.wait_ge(zf_done, m * 3 + (n + 1))
                    act.sem_inc(act_passed, 1)
                    act.copy(blk(hh, n, m), gcs[:, n, :]).then_inc(z_hi_done, 1)
                    if n == NG - 1:
                        split_next(2)

            def ln_square(i):
                act.wait_ge(centred, i + 1)
                act.activation(lnt[:], grp(acc, i % NG), ACT.Square).then_inc(squared, 1)

            def ln_std(i):
                act.wait_ge(var_copied, i + 1)
                wait(act, normed, i)
                act.activation(std[:], var[:], ACT.Sqrt).then_inc(std_done, 1)

            def ln_affine(i):
                stage, n = i // NG, i % NG
                act.wait_ge(normed, i + 1)
                for k in range(KD):
                    last = act.activation(blk(acc, n, k), blk(acc, n, k), ACT.Identity,
                                          bias=lnv(stage, 1, k), scale=lnv(stage, 0, k))
                last.then_inc(affine, 1)

            def ln_split(i):
                act.wait_ge(affine, i + 1)
                act.copy(grp(hh, i % NG), grp(acc, i % NG)).then_inc(ln_hi, 1)

            def gate(layer, half, i):
                a = half * 12 + i
                act.wait_ge(a_full, OUT_TILES + A_GATE[layer] + a + 1)
                if a >= 2:
                    act.wait_ge(b_free, BF_GATE[layer] + a - 1)
                elif layer == 1:
                    act.wait_ge(y_added, 24)
                act.activation(tt[:, a % 2, :], ps[:, a % 2, 0:TG], ACT.Sigmoid).then_inc(a_free, 1)

            def gates(layer):
                for half in range(2):
                    for i in range(12):
                        gate(layer, half, i)
                        if i >= 8:
                            mm = i - 8
                            if half == 0:
                                split_hi(("gate", layer, 4 + mm), mm)
                            else:
                                split_hi(("mlp", layer, 0, mm), mm)

            def relu2(layer, c, n, mm):
                per = NG * CHUNK
                t = layer * NCH * per + n * CHUNK + mm
                a = A_MLP[layer] + n * CHUNK + mm
                act.wait_ge(a_full, c * per + (OUT_TILES + a + 1))
                if isinstance(c, int) and c == 0 and n == 0:
                    act.wait_ge(b_free, BF_GATE[layer] + 24)
                else:
                    act.wait_ge(sq_done, c * per + (t - 1))
                act.activation(tt[:, a % 2, :], ps[:, a % 2, 0:TG], ACT.Relu).then_inc(a_free, 1)
                act.wait_ge(a_free, c * per + (a + 1))
                act.wait_ge(b_full, c * (NG * KD) + (B_MLP[layer] + (n + 1) * KD - NG * KD))
                act.activation(rpart(rh, n, mm), tt[:, a % 2, :], ACT.Square).then_inc(r_hi_done, 1)

            def mlp(layer):
                def split_next(c, j):
                    s, q, use = units["mlp", layer, 0, j]
                    act.wait_ge(raw_in[q], c * 16 + 16 * (use + 2))
                    act.copy(ws[:, j, 0, :], raw[:, q, :]).then_inc(w_hi, 1)

                relu2(layer, 0, 0, 0)
                relu2(layer, 0, 0, 1)
                with act.Fori(0, NCH - 1) as c:
                    relu2(layer, c, 1, 0)
                    relu2(layer, c, 1, 1)
                    relu2(layer, c, 2, 0)
                    split_next(c, 0)
                    relu2(layer, c, 2, 1)
                    split_next(c, 1)
                    relu2(layer, c + 1, 0, 0)
                    relu2(layer, c + 1, 0, 1)
                    act.wait_ge(b_full, c * (NG * KD) + (B_MLP[layer] + NG * KD))
                    split_next(c, 2)
                    split_next(c, 3)
                c = NCH - 1
                i = NG * (2 * layer + 1)
                for n in (1, 2):
                    relu2(layer, c, n, 0)
                    relu2(layer, c, n, 1)
                if layer == 0:
                    split_hi(("grp", 0), 4)
                    split_hi(("grp", 1), 5)
                    split_hi(("gate", 1, 0), 0)
                    split_hi(("gate", 1, 1), 1)
                ln_square(i)
                if layer == 0:
                    act.wait_ge(b_full, B_GRP)
                    split_hi(("gate", 1, 2), 2)
                    split_hi(("gate", 1, 3), 3)
                for n in range(NG):
                    ln_std(i + n)
                    if n + 1 < NG:
                        ln_square(i + n + 1)
                    ln_affine(i + n)
                    if layer == 0:
                        pool_group(n)
                        scale_group(n)

            def pool_group(n):
                act.wait_ge(affine, NG + n + 1)
                if n < NG - 1:
                    act.copy(tails[:, n, :, :], grp3(acc, n)[:, :, TG - HIST:TG]).then_inc(tail_saved, 1)
                for q in range(4):
                    w = n * 4 + q
                    ks = slice(2 * q, 2 * q + 2)
                    src = grp3(acc, n)[:, ks, :]
                    dst = wa[:, w % 2]
                    wait(act, d_ready, w - 1)
                    if n == 0:
                        act.copy(dst[:, :, 0:HIST], zeros[:])
                    else:
                        act.wait_ge(tail_saved, n)
                        act.copy(dst[:, :, 0:HIST], tails[:, n - 1, ks, :])
                    if n < NG - 1:
                        act.copy(dst[:, :, HIST:HIST + TG], src).then_inc(win_in, 1)
                    else:
                        act.copy(dst[:, :, HIST:HIST + TAIL], src[:, :, 0:TAIL])
                        act.copy(dst[:, :, HIST + TAIL:2 * HIST + TAIL], phist[:, ks, :])
                        act.copy(dst[:, :, 2 * HIST + TAIL:WIN], src[:, :, TAIL:TG]).then_inc(win_in, 1)
                    if q >= 1:
                        split_d(w - 1)
                split_d(n * 4 + 3)

            def split_d(w):
                n, q = w // 4, w % 4
                act.wait_ge(d_done, w + 1)
                for a, b, off in pieces(n):
                    last = act.copy(grp3(hh, n)[:, 2 * q:2 * q + 2, a:b], sums(w)[:, :, a + off:b + off])
                last.then_inc(d_hi_done, 1)

            def scale_group(n):
                for m in range(KD):
                    b = n * KD + m
                    act.wait_ge(b_full, B_GRP + b + 1)
                    if b >= 2:
                        act.wait_ge(y_added, b - 1)
                    else:
                        act.wait_ge(sq_done, NCH * NG * CHUNK)
                    act.mul(tt[:, b % 2, :], ps[:, B_BANK + b % 4, 0:TG],
                            vec[:, V_SCALE + m:V_SCALE + m + 1]).then_inc(y_scaled, 1)

            def finish_ln(i):
                ln_std(i)
                ln_affine(i)
                ln_split(i)

            split_x(0)
            for j in range(3):
                split_hi(("in", 0, j), j)
            split_x(1)
            split_x(2)
            act.wait_ge(setup, 3)
            act.wait_ge(small_in, 48)
            conv_in(0)
            with act.Fori(1, KD) as m:
                conv_in(m)
            split_hi(("out", 3), 3)
            for mm in range(4):
                act.wait_ge(a_full, 8 + mm + 1)
                split_hi(("out", 4 + mm), mm)
            act.wait_ge(z_ready, KD * NG)
            act.wait_ge(u_saved, KD)
            split_hi(("ple", 0, 0), 4)
            split_hi(("ple", 0, 1), 5)
            ln_square(0)
            act.wait_ge(a_full, 12 + 8 + 1)
            split_hi(("gate", 0, 0), 0)
            ln_std(0)
            act.wait_ge(a_full, 12 + 8 + 2)
            split_hi(("gate", 0, 1), 1)
            ln_affine(0)
            for mm in range(2, 4):
                act.wait_ge(a_full, 12 + 8 + mm + 1)
                split_hi(("gate", 0, mm), mm)
            ln_split(0)
            ln_square(1)
            act.wait_ge(out_added, OUT_TILES)
            for n in range(NG):
                split_p(0, n)
            ln_std(1)
            ln_square(2)
            ln_affine(1)
            ln_split(1)
            finish_ln(2)
            gates(0)
            mlp(0)
            ln_square(6)
            ln_std(6)
            ln_square(7)
            ln_affine(6)
            ln_split(6)
            act.wait_ge(d_ready, 12)
            act.wait_ge(b_full, B_GATE[1])
            split_hi(("ple", 1, 0), 4)
            split_hi(("ple", 1, 1), 5)
            for n in range(NG):
                split_p(1, n)
            ln_std(7)
            ln_square(8)
            ln_affine(7)
            ln_split(7)
            finish_ln(8)
            gates(1)
            mlp(1)

        @block.vector
        def _(dve):
            def split_lo(name, slot):
                s, q, _ = units[name]
                dve.wait_ge(w_hi, s + 1)
                dve.tensor_tensor(ws[:, slot, 1, :], raw[:, q, :], f32(ws[:, slot, 0, :]), ALU.subtract).then_inc(w_lo, 1)

            def split_p(layer, n):
                s, q, _ = units["p", layer, n]
                dve.wait_ge(w_hi, s + 1)
                cols = slice(n * KP * TG, (n + 1) * KP * TG)
                dve.tensor_tensor(rl[:, cols], raw[:, q, 0:KP * TG], f32(rh[:, cols]), ALU.subtract).then_inc(w_lo, 1)

            def split_x(n):
                dve.wait_ge(x_hi_done, n + 1)
                dve.tensor_tensor(grp(xl, n), grp(xraw, n), f32(grp(xh, n)), ALU.subtract).then_inc(x_ready, 1)

            def conv_in(m):
                def split_next(j):
                    dve.wait_ge(w_hi, m * 3 + (4 + j))
                    dve.tensor_tensor(ws[:, j, 1, :], raw[:, j, :], f32(ws[:, j, 0, :]), ALU.subtract).then_inc(w_lo, 1)

                def w(j):
                    return vec[:, m * 3 + j:m * 3 + j + 1] if isinstance(m, int) else vec[:, bass.ds(m * 3 + j, 1)]

                for n in range(NG):
                    q1 = m * 3 + (n + 1)
                    dve.wait_ge(h_full, q1)
                    dve.wait_ge(gc_copied, q1)
                    at = CH + n * TG
                    if n < NG - 1:
                        dve.tensor_tensor(ub[:, at:at + TG], gcs[:, n, :], ps[:, 1, 0:TG], ALU.mult).then_inc(u_done, 1)
                    else:
                        wait(dve, u_saved, m)
                        dve.tensor_tensor(ub[:, at:at + TAIL], gcs[:, n, 0:TAIL], ps[:, 1, 0:TAIL], ALU.mult)
                        dve.tensor_tensor(ub[:, UW - SAMPLE:UW], gcs[:, n, TAIL:TG], ps[:, 1, TAIL:TG],
                                          ALU.mult).then_inc(u_done, 1)
                        split_next(0)
                    width = TG if n < NG - 1 else CW
                    dve.wait_ge(tap0, q1)
                    dve.scalar_tensor_tensor(out=cv[:, n, 0:width], in0=ub[:, n * TG + 1:n * TG + 1 + width], scalar=w(1),
                                             in1=cv[:, n, 0:width], op0=ALU.mult, op1=ALU.add).then_inc(tap1, 1)
                    dve.wait_ge(tap1, q1)
                    w2 = width if n < NG - 1 else CW
                    dve.scalar_tensor_tensor(out=cv[:, n, 0:w2], in0=ub[:, n * TG + 2:n * TG + 2 + w2], scalar=w(2),
                                             in1=cv[:, n, 0:w2], op0=ALU.mult, op1=ALU.add).then_inc(tap2, 1)
                    if n == NG - 1:
                        split_next(1)
                    dve.wait_ge(tap2, q1)
                    dve.wait_ge(gb_full, q1)
                    if n < NG - 1:
                        dve.tensor_tensor(gcs[:, n, :], cv[:, n, 0:TG], ps[:, 2, 0:TG], ALU.mult).then_inc(zf_done, 1)
                    else:
                        dve.tensor_tensor(gcs[:, n, 0:TAIL], cv[:, n, 0:TAIL], ps[:, 2, 0:TAIL], ALU.mult)
                        dve.tensor_tensor(gcs[:, n, TAIL:TG], cv[:, n, TAIL + CH:CW], ps[:, 2, TAIL:TG],
                                          ALU.mult).then_inc(zf_done, 1)
                    dve.wait_ge(z_hi_done, q1)
                    dve.tensor_tensor(blk(hl, n, m), gcs[:, n, :], f32(blk(hh, n, m)), ALU.subtract).then_inc(z_ready, 1)
                    if n == NG - 1:
                        split_next(2)

            def conv_out(i):
                half, n, mm = i // 12, i // 4 % 3, i % 4
                m = 4 * half + mm
                dve.wait_ge(a_full, i + 1)
                dve.scalar_tensor_tensor(out=blk(acc, n, m), in0=f32(blk(xh, n, m)), scalar=ALPHA, in1=ps[:, i % 2, 0:TG],
                                         op0=ALU.mult, op1=ALU.add).then_inc(out_free, 1)
                dve.wait_ge(out_free, i + 1)
                dve.scalar_tensor_tensor(out=blk(acc, n, m), in0=f32(blk(xl, n, m)), scalar=ALPHA, in1=blk(acc, n, m),
                                         op0=ALU.mult, op1=ALU.add).then_inc(out_added, 1)

            steps = [0]

            def then(ins):
                steps[0] += 1
                ins.then_inc(ln_step, 1)
                dve.wait_ge(ln_step, steps[0])

            def tree(src, out, done):
                half = GCOLS // 2
                then(dve.tensor_tensor(lnt[:, 0:half], src[:, 0:half], src[:, half:2 * half], ALU.add))
                then(dve.tensor_tensor(lnt[:, 0:half // 2], lnt[:, 0:half // 2], lnt[:, half // 2:half], ALU.add))
                dve.tensor_tensor(out, lnt[:, 0:TG], lnt[:, TG:2 * TG], ALU.add).then_inc(done, 1)

            def ln_sum(i):
                wait(dve, mean_full, i)
                wait(dve, var_sum, i)
                tree(grp(acc, i % NG), s_mean[:], mean_sum)

            def over_blocks(ap):
                return ap.rearrange("p (a t) -> p a t", a=1).to_broadcast([P, KD, TG])

            def ln_centre(i):
                n = i % NG
                dve.wait_ge(mean_full, i + 1)
                dve.tensor_tensor(grp3(acc, n), grp3(acc, n), over_blocks(ps[:, MEAN_BANK, 0:TG]), ALU.subtract).then_inc(centred, 1)

            def ln_var(i):
                dve.wait_ge(squared, i + 1)
                wait(dve, var_full, i)
                tree(lnt[:], s_var[:], var_sum)

            def ln_norm(i):
                n = i % NG
                dve.wait_ge(var_full, i + 1)
                dve.tensor_scalar(var[:], ps[:, VAR_BANK, 0:TG], EPS, None, ALU.add).then_inc(var_copied, 1)
                dve.wait_ge(std_done, i + 1)
                then(dve.reciprocal(std[:], std[:]))
                then(dve.scalar_tensor_tensor(out=rstd[:], in0=std[:], scalar=-0.5, in1=std[:], op0=ALU.mult, op1=ALU.mult))
                dve.wait_ge(var_copied, i + 1)
                then(dve.tensor_tensor(rstd[:], rstd[:], var[:], ALU.mult))
                then(dve.scalar_tensor_tensor(out=rstd[:], in0=rstd[:], scalar=1.5, in1=std[:], op0=ALU.add, op1=ALU.mult))
                dve.tensor_tensor(grp3(acc, n), grp3(acc, n), over_blocks(rstd[:]), ALU.mult).then_inc(normed, 1)

            def ln_split(i):
                n = i % NG
                dve.wait_ge(ln_hi, (i // NG) // 2 * NG + n + 1)
                dve.tensor_tensor(grp(hl, n), grp(acc, n), f32(grp(hh, n)), ALU.subtract).then_inc(h_ready, 1)

            def gate(layer, half, i):
                n, mm = i // 4, i % 4
                m = 4 * half + mm
                g = half * 12 + i
                b = B_GATE[layer] + g
                dve.wait_ge(a_free, A_GATE[layer] + g + 1)
                dve.wait_ge(b_full, b + 1)
                dve.tensor_tensor(sq[:, g % 2, :], tt[:, g % 2, :], ps[:, B_BANK + g % 4, 0:TG], ALU.mult).then_inc(b_free, 1)
                dve.wait_ge(b_free, BF_GATE[layer] + g + 1)
                dve.scalar_tensor_tensor(out=blk(acc, n, m), in0=blk(acc, n, m), scalar=ALPHA, in1=sq[:, g % 2, :],
                                         op0=ALU.mult, op1=ALU.add).then_inc(gate_added, 1)

            def gates(layer):
                for half in range(2):
                    for i in range(12):
                        gate(layer, half, i)
                        if i >= 8:
                            mm = i - 8
                            split_lo(("gate", layer, 4 + mm) if half == 0 else ("mlp", layer, 0, mm), mm)
                dve.wait_ge(gate_added, 24 * (layer + 1))

            def relu2(layer, c, n, mm):
                per = NG * CHUNK
                t = layer * NCH * per + n * CHUNK + mm
                a = A_MLP[layer] + n * CHUNK + mm
                dve.wait_ge(a_free, c * per + (a + 1))
                dve.tensor_tensor(sq[:, a % 2, :], tt[:, a % 2, :], tt[:, a % 2, :], ALU.mult).then_inc(sq_done, 1)
                dve.wait_ge(sq_done, c * per + (t + 1))
                dve.wait_ge(r_hi_done, c * per + (t + 1))
                dve.tensor_tensor(rpart(rl, n, mm), sq[:, a % 2, :], f32(rpart(rh, n, mm)), ALU.subtract).then_inc(r_ready, 1)

            def add(layer, c, n, blocks=range(KD)):
                for m in blocks:
                    b = n * KD + m
                    dve.wait_ge(b_full, c * (NG * KD) + (B_MLP[layer] + b + 1))
                    dve.tensor_tensor(blk(acc, n, m), blk(acc, n, m), ps[:, B_BANK + b % 4, 0:TG], ALU.add).then_inc(b_free, 1)

            def mlp(layer):
                def split_next(c, j):
                    s, q, _ = units["mlp", layer, 0, j]
                    dve.wait_ge(w_hi, c * 4 + (s + 5))
                    dve.tensor_tensor(ws[:, j, 1, :], raw[:, q, :], f32(ws[:, j, 0, :]), ALU.subtract).then_inc(w_lo, 1)

                relu2(layer, 0, 0, 0)
                relu2(layer, 0, 0, 1)
                with dve.Fori(0, NCH - 1) as c:
                    relu2(layer, c, 1, 0)
                    relu2(layer, c, 1, 1)
                    add(layer, c, 0)
                    relu2(layer, c, 2, 0)
                    split_next(c, 0)
                    relu2(layer, c, 2, 1)
                    split_next(c, 1)
                    add(layer, c, 1)
                    relu2(layer, c + 1, 0, 0)
                    relu2(layer, c + 1, 0, 1)
                    add(layer, c, 2)
                    split_next(c, 2)
                    split_next(c, 3)
                c = NCH - 1
                i = NG * (2 * layer + 1)
                relu2(layer, c, 1, 0)
                relu2(layer, c, 1, 1)
                add(layer, c, 0)
                dve.wait_ge(b_free, BF_GATE[layer] + 24 + c * NG * KD + KD)
                ln_sum(i)
                relu2(layer, c, 2, 0)
                relu2(layer, c, 2, 1)
                if layer == 0:
                    split_lo(("grp", 0), 4)
                    split_lo(("grp", 1), 5)
                    split_lo(("gate", 1, 0), 0)
                    split_lo(("gate", 1, 1), 1)
                ln_centre(i)
                add(layer, c, 1)
                ln_var(i)
                add(layer, c, 2)
                if layer == 0:
                    split_lo(("gate", 1, 2), 2)
                    split_lo(("gate", 1, 3), 3)
                dve.wait_ge(b_free, BF_GATE[layer] + 24 + (c + 1) * NG * KD)
                for n in range(NG):
                    if n + 1 < NG:
                        ln_sum(i + n + 1)
                    ln_norm(i + n)
                    if n + 1 < NG:
                        ln_centre(i + n + 1)
                        ln_var(i + n + 1)
                    if layer == 0:
                        for q in range(4):
                            centre_pool(n * 4 + q)
                        add_grouped(n)

            d_steps = [0]

            def centre_pool(w):
                n, q = w // 4, w % 4
                res = sums(w)
                dve.wait_ge(win_done, w + 1)
                if n == 0:
                    at = V_RATIO + q * HIST
                    ratio = vec[:, at:at + HIST].rearrange("p (a t) -> p a t", a=1).to_broadcast([P, 2, HIST])
                    d_steps[0] += 1
                    dve.tensor_tensor(res[:, :, HIST:2 * HIST], res[:, :, HIST:2 * HIST], ratio, ALU.mult).then_inc(d_step, 1)
                    dve.wait_ge(d_step, d_steps[0])
                src = grp3(acc, n)[:, 2 * q:2 * q + 2, :]
                for a, b, off in pieces(n):
                    last = dve.scalar_tensor_tensor(out=res[:, :, a + off:b + off], in0=res[:, :, a + off:b + off],
                                                    scalar=1.0 / WINDOWS[q], in1=src[:, :, a:b], op0=ALU.mult, op1=ALU.subtract)
                last.then_inc(d_done, 1)
                dve.wait_ge(d_hi_done, w + 1)
                for a, b, off in pieces(n):
                    last = dve.tensor_tensor(grp3(hl, n)[:, 2 * q:2 * q + 2, a:b], res[:, :, a + off:b + off],
                                             f32(grp3(hh, n)[:, 2 * q:2 * q + 2, a:b]), ALU.subtract)
                last.then_inc(d_ready, 1)

            def add_grouped(n):
                if n == NG - 1:
                    dve.wait_ge(state_out, 32)
                for m in range(KD):
                    b = n * KD + m
                    dve.wait_ge(y_scaled, b + 1)
                    dve.scalar_tensor_tensor(out=blk(acc, n, m), in0=blk(acc, n, m), scalar=ALPHA, in1=tt[:, b % 2, :],
                                             op0=ALU.mult, op1=ALU.add).then_inc(y_added, 1)

            split_x(0)
            for j in range(3):
                split_lo(("in", 0, j), j)
            split_x(1)
            split_x(2)
            dve.wait_ge(small_in, 48)
            dve.wait_ge(setup, 3)
            conv_in(0)
            with dve.Fori(1, KD) as m:
                conv_in(m)
            split_lo(("out", 3), 3)
            for i in range(12):
                conv_out(i)
                if i >= 8:
                    split_lo(("out", 4 + i - 8), i - 8)
            split_lo(("ple", 0, 0), 4)
            split_lo(("ple", 0, 1), 5)
            for i in range(12, 16):
                conv_out(i)
            dve.wait_ge(out_added, 16)
            ln_sum(0)
            conv_out(16)
            conv_out(17)
            ln_centre(0)
            conv_out(18)
            conv_out(19)
            ln_var(0)
            conv_out(20)
            split_lo(("gate", 0, 0), 0)
            conv_out(21)
            ln_sum(1)
            ln_norm(0)
            split_lo(("gate", 0, 1), 1)
            conv_out(22)
            split_lo(("gate", 0, 2), 2)
            conv_out(23)
            split_lo(("gate", 0, 3), 3)
            ln_centre(1)
            ln_split(0)
            ln_var(1)
            dve.wait_ge(out_added, OUT_TILES)
            ln_sum(2)
            for n in range(NG):
                split_p(0, n)
            ln_norm(1)
            ln_centre(2)
            ln_var(2)
            ln_split(1)
            ln_norm(2)
            ln_split(2)
            gates(0)
            mlp(0)
            dve.wait_ge(y_added, 8)
            ln_sum(6)
            ln_centre(6)
            ln_var(6)
            dve.wait_ge(y_added, 24)
            ln_sum(7)
            ln_norm(6)
            ln_centre(7)
            ln_split(6)
            ln_var(7)
            ln_sum(8)
            split_lo(("ple", 1, 0), 4)
            split_lo(("ple", 1, 1), 5)
            for n in range(NG):
                split_p(1, n)
            ln_norm(7)
            ln_centre(8)
            ln_split(7)
            ln_var(8)
            ln_norm(8)
            ln_split(8)
            gates(1)
            mlp(1)

        @block.gpsimd
        def _(pool):
            pool.memset(ub[:, 0:CH], 0.0).then_inc(setup, 1)
            pool.memset(ones[:], 1.0 / D).then_inc(setup, 1)
            pool.memset(zeros[:], 0.0).then_inc(setup, 1)
            pool.wait_ge(small_in, 48)

            def state(m):
                static = isinstance(m, int)
                hist = chist[:, m * CH:(m + 1) * CH] if static else chist[:, bass.ds(m * CH, CH)]
                wait(pool, tap2, m * 3)
                pool.sem_inc(pool_passed, 1)
                pool.tensor_copy(ub[:, CH + PROMPT:2 * CH + PROMPT], hist).then_inc(hist_in, 1)
                pool.wait_ge(u_done, m * 3 + 3)
                pool.sem_inc(pool_passed, 1)
                for part, at in enumerate((PROMPT, UW - CH)):
                    col = m * 2 * CH + part * CH
                    dst = cnew[:, col:col + CH] if static else cnew[:, bass.ds(col, CH)]
                    last = pool.tensor_copy(dst, ub[:, at:at + CH])
                last.then_inc(u_saved, 1)

            state(0)
            with pool.Fori(1, KD) as m:
                state(m)

            n_steps = [0]
            for n in range(NG):
                for q, window in enumerate(WINDOWS):
                    w = n * 4 + q
                    src, dst = wa[:, w % 2], wb[:, w % 2]
                    pool.wait_ge(win_in, w + 1)
                    wait(pool, d_ready, w - 1)
                    lag, have = 1, 0
                    end = WIN if n == NG - 1 else HIST + TG
                    while lag < window:
                        have += lag
                        ins = pool.tensor_tensor(dst[:, :, have:end], src[:, :, have:end], src[:, :, have - lag:end - lag], ALU.add)
                        src, dst = dst, src
                        lag *= 2
                        if lag < window:
                            n_steps[0] += 1
                            ins.then_inc(win_step, 1)
                            pool.wait_ge(win_step, n_steps[0])
                    ins.then_inc(win_done, 1)


def kernel(**inputs):
    import numpy as np
    import concourse.bacc as bacc
    from concourse.bass_utils import run_bass_kernel_spmd

    def a(name):
        return np.asarray(inputs[name])

    def blocks(w):
        k, m = w.shape
        return w.reshape(k // P, P, m // P, P).transpose(2, 1, 0, 3).reshape(m // P, P, k)

    def activations(prompt, sample):
        t = np.concatenate([prompt, sample], axis=0)
        return t.reshape(NG, TG, -1, P).transpose(3, 0, 2, 1)

    w_in, w_out = blocks(a("a_w_in")[0]), blocks(a("a_w_out")[0])
    w1 = [blocks(a("mlp_w1")[i]) for i in range(DEPTH)]
    w2 = [a("mlp_w2")[i].reshape(FF // P, P, D) for i in range(DEPTH)]
    gate = [blocks(a("ple_gate_w")[i]) for i in range(DEPTH)]
    ple = [a("ple_w")[i].reshape(KP, P, D) for i in range(DEPTH)]
    groups = a("b_w_grp")[0].reshape(2, 2, 2, P, 256).transpose(0, 3, 1, 2, 4).reshape(2, P, U)
    stream = []
    units = weight_units()
    for name in sorted(units, key=lambda name: units[name][0]):
        kind = name[0]
        if kind == "in":
            stream.append(w_in[((1, 2, 0)[name[2]]) * KD + name[1]])
        elif kind == "out":
            stream.append(w_out[name[1]])
        elif kind == "ple":
            stream.append(ple[name[1]][name[2]])
        elif kind == "gate":
            stream.append(gate[name[1]][name[2]])
        elif kind == "grp":
            stream.append(groups[name[1]])
        elif kind == "mlp":
            _, i, c, j = name
            stream.append(w1[i][c * CHUNK + j] if j < CHUNK else w2[i][c * CHUNK + j - CHUNK])
    p_t = [activations(a("p_prompt")[i][0], a("p_sample")[i][0]).transpose(1, 0, 2, 3).reshape(NG * P, KP * TG) for i in range(DEPTH)]

    def features(v):
        return v.reshape(-1, KD, P).transpose(2, 0, 1).reshape(P, -1)

    conv_w = a("a_conv_w")[0].reshape(3, KD, P).transpose(2, 1, 0).reshape(P, 3 * KD)
    ln = np.stack([a("ln1_g")[0], a("ln1_b")[0], a("ln2_g")[0], a("ln2_b")[0],
                   a("ln1_g")[1], a("ln1_b")[1], a("ln2_g")[1], a("ln2_b")[1]])
    ratio = np.array([[w / min(t + 1, w) for t in range(HIST)] for w in WINDOWS], np.float32).reshape(1, -1)
    arrays = {
        "x_t": activations(a("x_prompt")[0], a("x_sample")[0]).reshape(P, NG * GCOLS),
        "w_stream": np.concatenate(stream, axis=0),
        "p_t": np.concatenate(p_t, axis=0),
        "vectors": np.concatenate([conv_w, features(a("b_scale")[0]), features(ln), np.broadcast_to(ratio, (P, ratio.size))], axis=1),
        "conv_hist": a("state_conv")[0, 0].reshape(CH, KD, P).transpose(2, 1, 0).reshape(P, KD * CH),
        "pool_hist": a("state_pool")[0, 0].reshape(HIST, KD, P).transpose(2, 1, 0).reshape(P, KD * HIST),
    }
    outs = {"y_t": (P, NG * GCOLS), "conv_new": (P, KD * 2 * CH), "pool_new": (P, KD, 2 * HIST)}

    nc = bacc.Bacc("TRN2", target_bir_lowering=False, num_devices=1)
    args = []
    for name, v in arrays.items():
        arrays[name] = v = np.ascontiguousarray(v)
        args.append(nc.dram_tensor(name, v.shape, F32, kind="ExternalInput").ap())
    for name, shape in outs.items():
        args.append(nc.dram_tensor(name, shape, F32, kind="ExternalOutput").ap())
    bass_streaming_trunk(nc, *args)
    r = run_bass_kernel_spmd(nc, [arrays], core_ids=[0]).results[0]

    y = np.asarray(r["y_t"]).reshape(P, NG, KD, TG).transpose(1, 3, 2, 0).reshape(TOKENS, D)
    conv = np.asarray(r["conv_new"]).reshape(P, KD, 2, CH).transpose(2, 3, 1, 0).reshape(2, CH, D)
    pool = np.asarray(r["pool_new"]).reshape(P, KD, 2, HIST).transpose(2, 3, 1, 0).reshape(2, HIST, D)
    return (y[None, :PROMPT], y[None, PROMPT:], conv[None, 0:1], conv[None, 1:2], pool[None, 0:1], pool[None, 1:2])
```

```python
from contextlib import ExitStack
from dataclasses import dataclass, field, replace

import concourse.bass as bass
from concourse import mybir

F32 = mybir.dt.float32
F32R = mybir.dt.float32r
ALU = mybir.AluOpType
ACT = mybir.ActivationFunctionType

P = 128
D = 1024
KD = D // P
PROMPT, SAMPLE = 1024, 32
TOKENS = PROMPT + SAMPLE
NG = 3
TG = TOKENS // NG
TAIL = PROMPT - (NG - 1) * TG
FF = 4 * D
CHUNK = 2
NCH = FF // P // CHUNK
PLE = 256
KP = PLE // P
WINDOWS = (2, 4, 8, 16)
HIST = 15
CH = 2
DEPTH = 2
ALPHA = (2 * DEPTH) ** 0.25
EPS = 1e-5
U = 1024
GCOLS = KD * TG


AHEAD = (5, 7)
BEHIND = 2
ALONE, PAIR, ALL = (0,), (1, 2), (0, 1, 2)
NORMS = [("mix", 0, 0), ("mix", 0, 1), ("mix", 0, 2),
         ("mlp", 0, 0), ("mix", 1, 0), ("mlp", 0, 1), ("mlp", 0, 2), ("mix", 1, 1), ("mix", 1, 2),
         ("mlp", 1, 0), ("mlp", 1, 1), ("mlp", 1, 2)]


@dataclass
class Unit:
    name: tuple
    row: int
    s: int
    q: int
    use: int
    by: str
    o: int
    before: object

    def later(self, i):
        before = self.before
        if before is not None:
            before = replace(before, o=i * 4 + before.o)
        return replace(self, s=i * 4 + self.s, use=i + self.use, o=i * 4 + self.o, row=i * 4 + self.row, before=before)


@dataclass
class Step:
    kind: str
    layer: int = 0
    n: int = 0
    m: int = 0
    blocks: object = None
    slot: int = 0
    part: int = 0
    a: int = 0
    b: int = 0
    bank: int = 0
    t: int = 0
    t_buf: int = 0
    t_free: object = None
    r_used: int = 0
    r_need: int = 0
    body: object = None
    passes: int = 0
    refill: list = field(default_factory=list)
    side: list = field(default_factory=list)
    need: list = field(default_factory=list)

    def later(self, i):
        a, b = i * (NG * CHUNK), i * (NG * KD)
        step = replace(self, a=a + self.a, b=b + self.b, t=a + self.t, r_used=b + self.r_used, r_need=a + self.r_need,
                       refill=[(u.later(i), slot, [(sem, b + v) for sem, v in conds]) for u, slot, conds in self.refill],
                       need=[u.later(i) for u in self.need])
        if self.kind == "up":
            step.t_free = (self.t_free[0], a + self.t_free[1])
        return step


def stream_rows():
    names = [("in", m, j) for m in range(KD) for j in range(3)] + [("out", m) for m in range(KD)] + [("grp", 0), ("grp", 1)]
    for layer in range(DEPTH):
        names += [("ple", layer, k) for k in range(KP)] + [("gate", layer, m) for m in range(KD)]
        names += [("mlp", layer, c, j) for c in range(NCH) for j in range(4)]
    return {name: row for row, name in enumerate(names)}


def number_units(plan):
    rows = stream_rows()
    uses, split_by, last_in, holds, total = [0] * 4, {"dve": 0, "pool": 0}, {}, {}, [0]

    def unit(name, by, q):
        u = Unit(name=name, row=rows.get(name, 0), s=total[0], q=q, use=uses[q], by=by, o=split_by[by], before=last_in.get(q))
        uses[q] += 1
        split_by[by] += 1
        total[0] += 1
        last_in[q] = u
        return u

    first = [unit(("in", m, j), "dve", j) for m in range(KD) for j in range(3)][:3]
    for j in range(3):
        holds[j] = unit(("out", j), "dve", j)
    q = [3]

    def take(steps):
        for step in steps:
            step.need = [holds[slot] for slot in step.need]
            if step.kind == "loop":
                take(step.body)
                for _ in range(4 * (step.passes - 1)):
                    unit(None, "dve", q[0])
                    q[0] = (q[0] + 1) % 4
                for slot in range(4):
                    holds[slot] = holds[slot].later(step.passes - 1)
                continue
            for i, (name, slot, conds, by) in enumerate(step.refill):
                holds[slot] = unit(name, by, q[0])
                q[0] = (q[0] + 1) % 4
                step.refill[i] = (holds[slot], slot, conds)
            step.side = [x[:-1] + (holds[x[-1]],) if x[0] == "grp" else x for x in step.side]

    take(plan)
    return first


def make_plan():
    plan = []
    count = {"out": 0, "a": 0, "b": 0, "t": 0, "gate": 0, "part": 0}
    t_free, r_used, filled = [None, None], {}, []

    def add(kind, **fields):
        plan.append(Step(kind, **fields))
        return plan[-1]

    def refill(step, name, slot, conds=(), by="dve"):
        step.refill.append((name, slot, list(conds), by))

    def inputs(step, layer, groups, conds):
        for n in groups:
            refill(step, ("p", layer, n), ("p", n), conds + [("b_full", r_used.get(n, 0))])

    def quads(groups, emit, names, following, by):
        for half in range(2):
            for n in groups:
                for mm in range(4):
                    step = emit(half, n, mm)
                    if n == groups[0]:
                        step.need = [mm]
                    if n == groups[-1]:
                        refill(step, names(4 + mm) if half == 0 else following[mm], mm, by=by(mm))

    def out_tile(half, n, mm):
        count["out"] += 1
        return add("out", n=n, m=4 * half + mm, slot=mm, a=count["out"] - 1)

    def gates(layer, groups, following, by):
        tiles = []

        def gate_tile(half, n, mm):
            a = count["a"]
            step = add("gate", layer=layer, n=n, m=4 * half + mm, slot=mm, a=a, bank=a % 2, t_free=t_free[a % 2])
            count["a"] += 1
            count["gate"] += 1
            t_free[a % 2] = ("gate_added", count["gate"])
            tiles.append(step)
            if len(tiles) >= 2:
                ple_tile(tiles[-2])
            return step

        def ple_tile(g):
            step = add("ple", n=g.n, m=g.m, t_buf=g.bank, a=g.a, b=count["b"], bank=count["b"] % 4)
            step.need = [4, 5, ("p", g.n)]
            count["b"] += 1
            r_used[g.n] = count["b"]

        quads(groups, gate_tile, lambda m: ("gate", layer, m), following, by)
        ple_tile(tiles[-1])

    def visits(layer, todo, following, by=lambda j: "dve", loop_at=None):

        def names(v):
            return [("mlp", layer, todo[v + 1][0], j) for j in range(4)] if v + 1 < len(todo) else following

        def splitter(v, j):
            return "dve" if todo[v][1] == ALL else by(j)

        def ups(v, n):
            part = count["part"] % NG
            count["part"] += 1
            filled.append([part, count["t"] + CHUNK])
            for mm in range(CHUNK):
                a, t = count["a"], count["t"]
                step = add("up", n=n, part=part, slot=mm, a=a, bank=a % 2, t=t, r_used=r_used[part], t_free=t_free[a % 2])
                count["a"], count["t"] = a + 1, t + 1
                t_free[a % 2] = ("r_ready", t + 1)
                if n == todo[v][1][0]:
                    step.need = [mm]
                if n == todo[v][1][-1] and names(v) is not None:
                    refill(step, names(v)[mm], mm, by=splitter(v, mm))

        def downs(v, n):
            part, ready = filled.pop(0)
            for blocks in (range(0, 4), range(4, 8)):
                step = add("down", n=n, part=part, blocks=blocks, b=count["b"], bank=count["b"] % 4, r_need=ready)
                if n == todo[v][1][0]:
                    step.need = [2, 3]
                count["b"] += len(blocks)
            r_used[part] = count["b"]
            if n == todo[v][1][-1] and names(v) is not None:
                for j in (2, 3):
                    refill(step, names(v)[j], j, [("b_full", count["b"])], splitter(v, j))

        ups(0, todo[0][1][0])
        v = 0
        while v < len(todo):
            begin, groups = len(plan), todo[v][1]
            for j in range(1, len(groups)):
                ups(v, groups[j])
                downs(v, groups[j - 1])
            if v + 1 < len(todo):
                ups(v + 1, todo[v + 1][1][0])
            downs(v, groups[-1])
            if v == loop_at:
                passes = 1
                while (todo[v + passes][1] == ALL and todo[v + passes + 1][0] == todo[v + passes][0] + 1
                       and todo[v + passes + 1][1][0] == 0 and len(todo[v + passes + 1][1]) > 1):
                    passes += 1
                    if v + passes + 1 >= len(todo):
                        break
                body = plan[begin:]
                del plan[begin:]
                add("loop", body=body, passes=passes)
                extra = passes - 1
                count["a"] += extra * NG * CHUNK
                count["t"] += extra * NG * CHUNK
                count["b"] += extra * NG * KD
                for n in ALL:
                    r_used[n] += extra * NG * KD
                filled[0][1] += extra * NG * CHUNK
                for x in range(2):
                    t_free[x] = (t_free[x][0], t_free[x][1] + extra * NG * CHUNK)
                v += extra
            v += 1

    def norm(i, done):
        n = NORMS.index(i)
        parts = [[("sum", n, done)], [("mean", n)], [("vsum", n)], [("var", n)], [("rstd", n)], [("norm", n)],
                 [("affine", n, 0)], [("affine", n, 1)]]
        return parts + ([[("hi", n)], [("lo", n)]] if i[0] == "mix" else [[], []])

    def two_norms(one, other, done_one, done_other):
        a, b = norm(one, done_one), norm(other, done_other)
        return [a[0], a[1], a[2], a[3], a[4], b[0], a[5], a[6] + b[1], a[7], b[2], b[3] + a[8], b[4], a[9], b[5],
                b[6], b[7], b[8], b[9]]

    def pooling(n):
        w = 4 * n

        def grp(j):
            return ("grp", 8 * n + j, 4 + j // 4)

        def add_(j):
            return ("gadd", 8 * n + j)

        return [[("fill", w)], [("fill", w + 1)], [("centre", w)], [("split", w), ("fill", w + 2)], [("centre", w + 1), grp(0)],
                [("split", w + 1), ("fill", w + 3), grp(1)], [("centre", w + 2), grp(2), add_(0)], [("split", w + 2), grp(3), add_(1)],
                [("centre", w + 3), grp(4), add_(2)], [("split", w + 3), grp(5), add_(3)], [grp(6), add_(4)], [grp(7), add_(5)],
                [add_(6), add_(7)]]

    def spread(steps, sides, dense=1):
        sides, steps = list(sides), [s for s in steps if s.kind not in ("ple", "refill")]
        for step in steps:
            for _ in range(dense):
                long = sides and any(x[0] in ("sum", "mean", "vsum", "rstd", "norm", "lo") for x in sides[0])
                if sides and not (long and step.kind == "down" and dense == 1):
                    step.side += sides.pop(0)
        for side in sides:
            plan[-1].side += side

    dve, both = (lambda j: "dve"), (lambda j: ("dve", "pool")[j % 2])
    gate0, gate1 = ([("gate", layer, m) for m in range(4)] for layer in range(DEPTH))
    mlp0, mlp1 = ([("mlp", layer, 0, j) for j in range(4)] for layer in range(DEPTH))

    start = add("refill")
    refill(start, ("out", 3), 3)
    conv_done = [("z_ready", KD * NG), ("u_saved", KD)]
    refill(start, ("ple", 0, 0), 4, conv_done)
    refill(start, ("ple", 0, 1), 5, conv_done)
    quads(ALONE, out_tile, lambda m: ("out", m), [("out", m) for m in range(4)], dve)
    here = len(plan)
    quads(PAIR, out_tile, lambda m: ("out", m), gate0, dve)
    spread(plan[here:here + 12], norm(("mix", 0, 0), ("out_added", 8)))
    others = two_norms(("mix", 0, 1), ("mix", 0, 2), ("out_added", 20), ("out_added", 24))
    spread(plan[here + 12:], others[:4])
    inputs(add("refill"), 0, ALL, [("out_added", 24)])
    here = len(plan)
    gates(0, ALONE, gate0, both)
    spread(plan[here:], others[4:], dense=2)
    gates(0, PAIR, mlp0, dve)
    ple_used = [("b_full", count["b"])]
    ahead = AHEAD[0]
    todo = [(c, ALL) for c in range(NCH - ahead)]
    todo += [(c, ALONE) for c in range(NCH - ahead, NCH)] + [(c, PAIR) for c in range(NCH - ahead, NCH)]
    visits(0, todo, gate1, both, loop_at=1)

    here = max(i for i, s in enumerate(plan) if s.kind == "down" and s.n == 0)
    for j in range(2):
        refill(plan[here], ("grp", j), 4 + j, ple_used)
    spread(plan[here:], norm(("mlp", 0, 0), ("b_free", plan[here].b + 4)) + pooling(0) + norm(("mix", 1, 0), ("y_added", 8)))
    done = [("b_free", s.b + 4) for n in PAIR for s in [[s for s in plan if s.kind == "down" and s.n == n][-1]]]
    step = add("refill")
    refill(step, ("ple", 1, 0), 4, [("grp_full", 8)])
    refill(step, ("ple", 1, 1), 5, [("grp_full", 8)])
    inputs(step, 1, ALONE, [])
    here = len(plan)
    gates(1, ALONE, mlp1, both)
    step = add("refill")
    for j in range(2):
        refill(step, ("grp", j), 4 + j, [("b_full", count["b"])])
    ahead, behind = AHEAD[1], BEHIND
    visits(1, [(c, ALONE) for c in range(ahead)], gate1, both)
    spread(plan[here:], two_norms(("mlp", 0, 1), ("mlp", 0, 2), *done) + join(pooling(1), pooling(2), 10)
           + two_norms(("mix", 1, 1), ("mix", 1, 2), ("y_added", 16), ("y_added", 24)), dense=2)
    step = add("refill")
    refill(step, ("ple", 1, 0), 4, [("grp_full", 24)])
    refill(step, ("ple", 1, 1), 5, [("grp_full", 24)])
    inputs(step, 1, PAIR, [])
    gates(1, PAIR, mlp1, dve)
    todo = [(c, PAIR) for c in range(ahead)] + [(c, ALL) for c in range(ahead, NCH - behind)]
    todo += [(c, (0, 1)) for c in range(NCH - behind, NCH)] + [(c, (2,)) for c in range(NCH - behind, NCH)]
    visits(1, todo, None, both, loop_at=ahead + 1)
    here = max(i for i, s in enumerate(plan) if s.kind == "down" and s.n == 1)
    done = [("b_free", [s for s in plan if s.kind == "down" and s.n == n][-1].b + 4) for n in ALL]
    last = two_norms(("mlp", 1, 0), ("mlp", 1, 1), done[0], done[1])
    spread(plan[here:], last, dense=2)
    step = add("rest")
    for side in norm(("mlp", 1, 2), done[2]):
        step.side += side
    return plan


def join(one, other, lag):
    out = [list(x) for x in one] + [[] for _ in range(max(0, lag + len(other) - len(one)))]
    for i, x in enumerate(other):
        out[lag + i] += x
    return out


def bass_streaming_trunk(nc, x_t, w_stream, p_t, vectors, conv_hist, pool_hist, y_t, conv_new, pool_new):
    plan = make_plan()
    first_units = number_units(plan)
    V_SCALE, V_LN, V_RATIO = 3 * KD, 4 * KD, 4 * KD + 4 * 2 * KD
    NV = V_RATIO + len(WINDOWS) * HIST

    with ExitStack() as ctx:
        cursor = [-(-nc.sbuf_base // 32) * 32]

        def place(name, shape, dt, at=None):
            size = 4
            for n in shape[1:]:
                size *= n
            size = -(-size // 32) * 32
            if at is None:
                at = cursor[0]
                cursor[0] += size
            return nc.alloc_sbuf_tensor_at(name, shape, dt, offset=at), at + size

        def sem(name):
            sems[name] = ctx.enter_context(nc.semaphore(name))
            return sems[name]

        sems = {}

        big = [P, NG * GCOLS]
        at1 = cursor[0]
        xh, _ = place("x_hi", big, F32R)
        acc, _ = place("acc", big, F32, at1)
        at2 = cursor[0]
        xl, end2 = place("x_lo", big, F32R)
        lnt, at3 = place("ln_squares", [P, GCOLS], F32, at2)
        WIN = HIST + TG + HIST
        w0, at = place("win_0", [P, 2, WIN], F32, at2)
        w1, at = place("win_1", [P, 2, WIN], F32, at)
        w2, at = place("win_2", [P, 2, WIN], F32, at)
        assert at <= at3
        rh, at = place("r_hi", [P, NG * CHUNK * TG], F32R, at3)
        rl, at = place("r_lo", [P, NG * CHUNK * TG], F32R, at)
        tt, at = place("t", [P, 2, TG], F32, at)
        gs, at = place("y_scaled_t", [P, 2, TG], F32, at)
        assert at <= end2
        hh, at6 = place("h_hi", big, F32R)
        hl, at7 = place("h_lo", big, F32R)
        xraw, _ = place("x_raw", big, F32, at6)
        ws, _ = place("w_split", [P, 6, 2, U], F32R)
        UW = CH + PROMPT + CH + SAMPLE
        CW = TG + CH
        ub, at = place("u", [P, UW], F32, at7 + 4 * 2 * U * 4)
        gcs, at = place("gc", [P, NG, TG], F32, at)
        cv, at = place("conv", [P, NG, CW], F32, at)
        assert at <= at7 + 6 * 2 * U * 4
        raw, _ = place("w_raw", [P, 4, U], F32)
        w3, _ = place("win_3", [P, 2, WIN], F32)
        ones, _ = place("ones", [P, P], F32)
        vec, _ = place("vec", [P, NV], F32)
        zeros, _ = place("zeros", [P, 2, HIST], F32)
        chist, _ = place("conv_history", [P, KD * CH], F32)
        phist, _ = place("pool_history", [P, KD, HIST], F32)
        cnew, _ = place("conv_state", [P, KD * 2 * CH], F32)
        tails, _ = place("tails", [P, 2, KD, HIST], F32)
        s_mean, _ = place("sum_mean", [P, TG], F32)
        s_var, at = place("sum_var", [P, TG], F32)
        std, _ = place("std", [P, TG], F32, at - -(-TG * 4 // 32) * 32)
        var, _ = place("var", [P, TG], F32)
        rstd, _ = place("rstd", [P, TG], F32)
        assert cursor[0] <= nc.sbuf_usable_end, (cursor[0], nc.sbuf_usable_end)
        wa, wb = (w0, w1), (w2, w3)
        ps = ctx.enter_context(nc.psum_tensor("ps", [P, 8, 512], F32))
        LN_BANK, B_BANK, GRP_BANK = 2, 3, 7

        x_in = [[sem(f"x_in{n}_{h}") for h in range(2)] for n in range(NG)]
        small_in = sem("small_in")
        raw_in = [sem(f"raw_in{q}") for q in range(4)]
        out_done, state_out = sem("out_done"), sem("state_out")
        w_hi = sem("w_hi")
        w_lo = {"dve": sem("w_lo_dve"), "pool": sem("w_lo_pool")}
        x_hi_done, x_ready, setup = sem("x_hi_done"), sem("x_ready"), sem("setup")
        act_passed, pool_passed = sem("act_passed"), sem("pool_passed")
        gc_full, h_full, gb_full = sem("gc_full"), sem("h_full"), sem("gb_full")
        gc_copied, u_done, tap0, tap1, tap2 = (sem(n) for n in ("gc_copied", "u_done", "tap0", "tap1", "tap2"))
        zf_done, z_hi_done, z_ready = sem("zf_done"), sem("z_hi_done"), sem("z_ready")
        hist_in, u_saved = sem("hist_in"), sem("u_saved")
        out_full, out_free, out_added = sem("out_full"), sem("out_free"), sem("out_added")
        a_full, a_free, b_full, b_free = sem("a_full"), sem("a_free"), sem("b_full"), sem("b_free")
        e_done, gate_added = sem("e_done"), sem("gate_added")
        t_squared, r_hi_done, r_ready = sem("t_squared"), sem("r_hi_done"), sem("r_ready")
        win_in, win_done, d_done, d_hi_done, d_ready = (sem(n) for n in ("win_in", "win_done", "d_done", "d_hi_done", "d_ready"))
        win_step, d_step = sem("win_step"), sem("d_step")
        grp_full, y_scaled, y_added, tail_saved = sem("grp_full"), sem("y_scaled"), sem("y_added"), sem("tail_saved")
        mean_sum, var_sum, mean_full, var_full = (sem(n) for n in ("mean_sum", "var_sum", "mean_full", "var_full"))
        centred, squared, var_copied, std_done, rstd_done, normed, affine, ln_hi, h_ready, ln_step = (
            sem(n) for n in ("centred", "squared", "var_copied", "std_done", "rstd_done", "normed", "affine", "ln_hi", "h_ready",
                             "ln_step"))

        block = ctx.enter_context(nc.Block())

        def wait(eng, s, value):
            if not isinstance(value, int) or value > 0:
                eng.wait_ge(s, value)

        def blk(t, n, k):
            at = n * GCOLS + k * TG
            return t[:, at:at + TG] if isinstance(at, int) else t[:, bass.ds(at, TG)]

        def grp(t, n):
            return t[:, n * GCOLS:(n + 1) * GCOLS]

        def half(t, n, h):
            return t[:, n * GCOLS + h * GCOLS // 2:n * GCOLS + (h + 1) * GCOLS // 2]

        def grp3(t, n):
            return grp(t, n).rearrange("p (k t) -> p k t", k=KD)

        def f32(ap):
            return ap.bitcast(F32)

        def rpart(t, n, f):
            at = (n * CHUNK + f) * TG
            return t[:, at:at + TG]

        def vcol(at):
            return vec[:, at:at + 1]

        def pieces(n):
            return ((0, TG, HIST),) if n < NG - 1 else ((0, TAIL, HIST), (TAIL, TG, 2 * HIST))

        def sums(w):
            return (wb if w % 2 == 0 else wa)[w % 2]

        def norm_of(i):
            kind, layer, n = NORMS[i]
            return kind, layer, n, (2 * layer + (kind == "mlp")) * 2 * KD + V_LN

        def mixed(i):
            return sum(k == "mix" for k, _, _ in NORMS[:i + 1])

        def subtract_hi(eng, u, slot):
            if isinstance(slot, tuple):
                cols = slice(slot[1] * KP * TG, (slot[1] + 1) * KP * TG)
                ins = eng.tensor_tensor(rl[:, cols], raw[:, u.q, 0:KP * TG], f32(rh[:, cols]), ALU.subtract)
            else:
                ins = eng.tensor_tensor(ws[:, slot, 1, :], raw[:, u.q, :], f32(ws[:, slot, 0, :]), ALU.subtract)
            ins.then_inc(w_lo[u.by], 1)

        def walk(eng, steps, do):
            for step in steps:
                if step.kind == "loop":
                    with eng.Fori(0, step.passes) as i:
                        for inner in step.body:
                            do(inner.later(i))
                else:
                    do(step)

        @block.sync
        def _(sp):
            def load(u):
                if u.before is not None:
                    sp.wait_ge(w_lo[u.before.by], u.before.o + 1)
                if u.name is not None and u.name[0] == "p":
                    row = (u.name[1] * NG + u.name[2]) * P
                    sp.dma_start(raw[:, u.q, 0:KP * TG], p_t[row:row + P, :]).then_inc(raw_in[u.q], 16)
                else:
                    at = u.row * P
                    src = w_stream[at:at + P, :] if isinstance(at, int) else w_stream[bass.ds(at, P), :]
                    sp.dma_start(raw[:, u.q, :], src).then_inc(raw_in[u.q], 16)

            def x_load(n, h):
                sp.dma_start(half(xraw, n, h), half(x_t, n, h)).then_inc(x_in[n][h], 16)

            x_load(0, 0)
            load(first_units[0])
            x_load(0, 1)
            load(first_units[1])
            load(first_units[2])
            sp.dma_start(vec[:], vectors).then_inc(small_in, 16)
            sp.dma_start(chist[:], conv_hist).then_inc(small_in, 16)
            sp.dma_start(phist[:], pool_hist.rearrange("p (k t) -> p k t", k=KD)).then_inc(small_in, 16)
            for n in range(1, NG):
                for h in range(2):
                    x_load(n, h)
            with sp.Fori(1, KD + 1) as m:
                for j in range(3):
                    sp.wait_ge(w_lo["dve"], m * 3 + (j - 2))
                    sp.dma_start(raw[:, j, :], w_stream[bass.ds((m * 3 + j) * P, P), :]).then_inc(raw_in[j], 16)

            def do(step):
                for u, _, _ in step.refill:
                    load(u)

            walk(sp, plan, do)
            sp.wait_ge(u_saved, KD)
            sp.dma_start(conv_new, cnew[:]).then_inc(out_done, 16)
            for n in range(NG):
                for h in range(2):
                    sp.wait_ge(affine, (len(NORMS) - NG + n) * 2 + h + 1)
                    sp.dma_start(half(y_t, n, h), half(acc, n, h)).then_inc(out_done, 16)
            sp.wait_ge(out_done, 16 * (2 * NG + 1))
            sp.wait_ge(state_out, 32)

        @block.tensor
        def _(pe):
            def triple(out, slot, col, mov_h, mov_l, first, last):
                wh, wl = ws[:, slot, 0, col:col + P], ws[:, slot, 1, col:col + P]
                pe.matmul(out, wh, mov_h, start=first, stop=False)
                pe.matmul(out, wh, mov_l, start=False, stop=False)
                return pe.matmul(out, wl, mov_h, start=False, stop=last)

            def full_tile(bank, slot, src_h, src_l, n):
                for k in range(KD):
                    mm = triple(ps[:, bank, 0:TG], slot, k * P, blk(src_h, n, k), blk(src_l, n, k), k == 0, k == KD - 1)
                return mm

            def conv_in(m):
                for n in range(NG):
                    for j, (full, freed) in enumerate(((gc_full, gc_copied), (h_full, u_done), (gb_full, zf_done))):
                        if n == 0:
                            wait(pe, w_lo["dve"], m * 3 + (j + 1))
                        wait(pe, freed, m * 3 + n)
                        for k in range(KD):
                            if isinstance(m, int) and j == 0 and k % (KD // 2) == 0:
                                pe.wait_ge(x_ready, n * 2 + k // (KD // 2) + 1)
                            mm = triple(ps[:, j, 0:TG], j, k * P, blk(xh, n, k), blk(xl, n, k), k == 0, k == KD - 1)
                        mm.then_inc(full, 1)

            def side(what, i, *rest):
                if what == "mean":
                    pe.wait_ge(mean_sum, i + 1)
                    wait(pe, var_copied, i)
                    pe.matmul(ps[:, LN_BANK, 0:TG], ones[:], s_mean[:], start=True, stop=True).then_inc(mean_full, 1)
                elif what == "var":
                    pe.wait_ge(var_sum, i + 1)
                    pe.wait_ge(centred, i + 1)
                    pe.matmul(ps[:, LN_BANK, 0:TG], ones[:], s_var[:], start=True, stop=True).then_inc(var_full, 1)
                elif what == "grp":
                    n, m = i // KD, i % KD
                    q = m // 2
                    pe.wait_ge(w_lo[rest[0].by], rest[0].o + 1)
                    pe.wait_ge(d_ready, n * 4 + q + 1)
                    wait(pe, y_scaled, i)
                    for k in range(2):
                        col = ((q % 2) * 2 + k) * 256 + (m % 2) * P
                        last = triple(ps[:, GRP_BANK, 0:TG], 4 + q // 2, col, blk(hh, n, 2 * q + k), blk(hl, n, 2 * q + k),
                                      k == 0, k == 1)
                    last.then_inc(grp_full, 1)

            def do(step):
                for u in step.need:
                    pe.wait_ge(w_lo[u.by], u.o + 1)
                if step.kind == "out":
                    wait(pe, out_free, step.a - 1)
                    full_tile(step.a % 2, step.slot, hh, hl, step.n).then_inc(out_full, 1)
                elif step.kind == "gate":
                    if step.m == 0:
                        pe.wait_ge(h_ready, step.layer * NG + step.n + 1)
                    if step.a < 2:
                        pe.wait_ge(out_free, 24)
                    else:
                        pe.wait_ge(a_free, step.a - 1)
                    full_tile(step.bank, step.slot, hh, hl, step.n).then_inc(a_full, 1)
                elif step.kind == "ple":
                    wait(pe, b_free, step.b - 3)
                    for k in range(KP):
                        last = triple(ps[:, B_BANK + step.bank, 0:TG], 4 + k, step.m * P, rpart(rh, step.n, k), rpart(rl, step.n, k),
                                      k == 0, k == KP - 1)
                    last.then_inc(b_full, 1)
                elif step.kind == "up":
                    pe.wait_ge(a_free, step.a - 1)
                    full_tile(step.bank, step.slot, hh, hl, step.n).then_inc(a_full, 1)
                elif step.kind == "down":
                    pe.wait_ge(r_ready, step.r_need)
                    for i, m in enumerate(step.blocks):
                        pe.wait_ge(b_free, step.b + (i - 3))
                        for f in range(CHUNK):
                            last = triple(ps[:, B_BANK + (step.bank + i) % 4, 0:TG], 2 + f, m * P, rpart(rh, step.part, f),
                                          rpart(rl, step.part, f), f == 0, f == CHUNK - 1)
                        last.then_inc(b_full, 1)
                for x in step.side:
                    side(*x)

            pe.wait_ge(setup, 3)
            conv_in(0)
            with pe.Fori(1, KD) as m:
                conv_in(m)
            pe.wait_ge(z_ready, KD * NG)
            walk(pe, plan, do)

        @block.scalar
        def _(act):
            def split_hi(u, slot, conds=()):
                act.wait_ge(raw_in[u.q], u.use * 16 + 16)
                for name, value in conds:
                    wait(act, sems[name], value)
                if isinstance(slot, tuple):
                    n = slot[1]
                    act.copy(rh[:, n * KP * TG:(n + 1) * KP * TG], raw[:, u.q, 0:KP * TG]).then_inc(w_hi, 1)
                else:
                    act.copy(ws[:, slot, 0, :], raw[:, u.q, :]).then_inc(w_hi, 1)

            def split_x(n, h):
                act.wait_ge(x_in[n][h], 16)
                act.copy(half(xh, n, h), half(xraw, n, h)).then_inc(x_hi_done, 1)

            def conv_in(m):
                def split_next(j):
                    act.wait_ge(raw_in[j], m * 16 + 32)
                    act.copy(ws[:, j, 0, :], raw[:, j, :]).then_inc(w_hi, 1)

                for n in range(NG):
                    act.wait_ge(gc_full, m * 3 + (n + 1))
                    wait(act, z_ready, m * 3 + (n - 2))
                    act.copy(gcs[:, n, :], ps[:, 0, 0:TG]).then_inc(gc_copied, 1)
                    if n == NG - 1:
                        split_next(0)
                        act.wait_ge(hist_in, m + 1)
                    act.wait_ge(u_done, m * 3 + (n + 1))
                    act.sem_inc(act_passed, 1)
                    width = TG if n < NG - 1 else CW
                    w0 = vec[:, bass.ds(m * 3, 1)] if not isinstance(m, int) else vec[:, m * 3:m * 3 + 1]
                    act.mul(cv[:, n, 0:width], ub[:, n * TG:n * TG + width], w0).then_inc(tap0, 1)
                    if n == NG - 1:
                        split_next(1)
                    act.wait_ge(zf_done, m * 3 + (n + 1))
                    act.sem_inc(act_passed, 1)
                    act.copy(blk(hh, n, m), gcs[:, n, :]).then_inc(z_hi_done, 1)
                    if n == NG - 1:
                        split_next(2)

            def side(what, i, *rest):
                if what == "mean":
                    act.wait_ge(centred, i + 1)
                    act.activation(lnt[:], grp(acc, NORMS[i][2]), ACT.Square).then_inc(squared, 1)
                elif what == "var":
                    act.wait_ge(var_copied, i + 1)
                    wait(act, rstd_done, i)
                    act.activation(std[:], var[:], ACT.Sqrt).then_inc(std_done, 1)
                elif what == "affine":
                    kind, layer, n, at = norm_of(i)
                    h, = rest
                    act.wait_ge(normed, i + 1)
                    for k in range(4 * h, 4 * h + 4):
                        last = act.activation(blk(acc, n, k), blk(acc, n, k), ACT.Identity, bias=vcol(at + KD + k), scale=vcol(at + k))
                    last.then_inc(affine, 1)
                    if (kind, layer, h) == ("mlp", 0, 1):
                        act.wait_ge(affine, 2 * i + 2)
                        if n < NG - 1:
                            act.copy(tails[:, n, :, :], grp3(acc, n)[:, :, TG - HIST:TG]).then_inc(tail_saved, 1)
                        else:
                            a2 = grp3(acc, n)
                            act.dma_start(pool_new[:, :, 0:HIST], a2[:, :, TAIL - HIST:TAIL]).then_inc(state_out, 16)
                            act.dma_start(pool_new[:, :, HIST:2 * HIST], a2[:, :, TG - HIST:TG]).then_inc(state_out, 16)
                elif what == "hi":
                    kind, layer, n, _ = norm_of(i)
                    act.wait_ge(affine, 2 * i + 2)
                    if layer == 0:
                        act.wait_ge(out_full, (8, 20, 24)[n])
                    act.copy(grp(hh, n), grp(acc, n)).then_inc(ln_hi, 1)
                elif what == "fill":
                    n, q = i // 4, i % 4
                    ks = slice(2 * q, 2 * q + 2)
                    src, dst = grp3(acc, n)[:, ks, :], wa[i % 2]
                    act.wait_ge(affine, 2 * NORMS.index(("mlp", 0, n)) + 2)
                    act.wait_ge(var_sum, NORMS.index(("mlp", 0, max(n, 2 * (n > 0)))) + 1)
                    wait(act, d_ready, i - 1)
                    if n == 0:
                        act.copy(dst[:, :, 0:HIST], zeros[:])
                    else:
                        act.wait_ge(tail_saved, n)
                        act.copy(dst[:, :, 0:HIST], tails[:, n - 1, ks, :])
                    if n < NG - 1:
                        act.copy(dst[:, :, HIST:HIST + TG], src).then_inc(win_in, 1)
                    else:
                        act.copy(dst[:, :, HIST:HIST + TAIL], src[:, :, 0:TAIL])
                        act.copy(dst[:, :, HIST + TAIL:2 * HIST + TAIL], phist[:, ks, :])
                        act.copy(dst[:, :, 2 * HIST + TAIL:WIN], src[:, :, TAIL:TG]).then_inc(win_in, 1)
                elif what == "centre":
                    n, q = i // 4, i % 4
                    act.wait_ge(d_done, i + 1)
                    for a, b, off in pieces(n):
                        last = act.copy(grp3(hh, n)[:, 2 * q:2 * q + 2, a:b], sums(i)[:, :, a + off:b + off])
                    last.then_inc(d_hi_done, 1)
                elif what == "grp":
                    m = i % KD
                    act.wait_ge(grp_full, i + 1)
                    wait(act, y_added, i - 1)
                    act.mul(gs[:, i % 2, :], ps[:, GRP_BANK, 0:TG], vcol(V_SCALE + m)).then_inc(y_scaled, 1)

            def do(step):
                if step.kind == "gate":
                    act.wait_ge(a_full, step.a + 1)
                    if step.t_free is not None:
                        act.wait_ge(sems[step.t_free[0]], step.t_free[1])
                    act.activation(tt[:, step.bank, :], ps[:, step.bank, 0:TG], ACT.Sigmoid).then_inc(a_free, 1)
                elif step.kind == "up":
                    t = tt[:, step.bank, :]
                    act.wait_ge(a_full, step.a + 1)
                    act.wait_ge(sems[step.t_free[0]], step.t_free[1])
                    act.activation(t, ps[:, step.bank, 0:TG], ACT.Relu).then_inc(a_free, 1)
                    act.wait_ge(a_free, step.a + 1)
                    act.activation(t, t, ACT.Square).then_inc(t_squared, 1)
                    act.wait_ge(t_squared, step.t + 1)
                    act.wait_ge(b_full, step.r_used)
                    act.copy(rpart(rh, step.part, step.slot), t).then_inc(r_hi_done, 1)
                for u, slot, conds in step.refill:
                    if step.kind == "out":
                        act.wait_ge(out_full, step.a + 1)
                    split_hi(u, slot, conds)
                for x in step.side:
                    side(*x)

            split_x(0, 0)
            split_hi(first_units[0], 0)
            split_x(0, 1)
            split_hi(first_units[1], 1)
            split_hi(first_units[2], 2)
            for n in range(1, NG):
                for h in range(2):
                    split_x(n, h)
            act.wait_ge(setup, 3)
            act.wait_ge(small_in, 48)
            conv_in(0)
            with act.Fori(1, KD) as m:
                conv_in(m)
            walk(act, plan, do)

        @block.vector
        def _(dve):
            def split_lo(u, slot):
                if u.by == "dve":
                    dve.wait_ge(w_hi, u.s + 1)
                    subtract_hi(dve, u, slot)

            def split_x(n, h):
                dve.wait_ge(x_hi_done, n * 2 + h + 1)
                dve.tensor_tensor(half(xl, n, h), half(xraw, n, h), f32(half(xh, n, h)), ALU.subtract).then_inc(x_ready, 1)

            def conv_in(m):
                def split_next(j):
                    dve.wait_ge(w_hi, m * 3 + (4 + j))
                    dve.tensor_tensor(ws[:, j, 1, :], raw[:, j, :], f32(ws[:, j, 0, :]), ALU.subtract).then_inc(w_lo["dve"], 1)

                def w(j):
                    return vec[:, m * 3 + j:m * 3 + j + 1] if isinstance(m, int) else vec[:, bass.ds(m * 3 + j, 1)]

                for n in range(NG):
                    q1 = m * 3 + (n + 1)
                    dve.wait_ge(h_full, q1)
                    dve.wait_ge(gc_copied, q1)
                    at = CH + n * TG
                    if n < NG - 1:
                        dve.tensor_tensor(ub[:, at:at + TG], gcs[:, n, :], ps[:, 1, 0:TG], ALU.mult).then_inc(u_done, 1)
                    else:
                        wait(dve, u_saved, m)
                        dve.tensor_tensor(ub[:, at:at + TAIL], gcs[:, n, 0:TAIL], ps[:, 1, 0:TAIL], ALU.mult)
                        dve.tensor_tensor(ub[:, UW - SAMPLE:UW], gcs[:, n, TAIL:TG], ps[:, 1, TAIL:TG],
                                          ALU.mult).then_inc(u_done, 1)
                        split_next(0)
                    width = TG if n < NG - 1 else CW
                    for tap, before, done in ((1, tap0, tap1), (2, tap1, tap2)):
                        dve.wait_ge(before, q1)
                        dve.scalar_tensor_tensor(out=cv[:, n, 0:width], in0=ub[:, n * TG + tap:n * TG + tap + width], scalar=w(tap),
                                                 in1=cv[:, n, 0:width], op0=ALU.mult, op1=ALU.add).then_inc(done, 1)
                    if n == NG - 1:
                        split_next(1)
                    dve.wait_ge(tap2, q1)
                    dve.wait_ge(gb_full, q1)
                    if n < NG - 1:
                        dve.tensor_tensor(gcs[:, n, :], cv[:, n, 0:TG], ps[:, 2, 0:TG], ALU.mult).then_inc(zf_done, 1)
                    else:
                        dve.tensor_tensor(gcs[:, n, 0:TAIL], cv[:, n, 0:TAIL], ps[:, 2, 0:TAIL], ALU.mult)
                        dve.tensor_tensor(gcs[:, n, TAIL:TG], cv[:, n, TAIL + CH:CW], ps[:, 2, TAIL:TG],
                                          ALU.mult).then_inc(zf_done, 1)
                    dve.wait_ge(z_hi_done, q1)
                    dve.tensor_tensor(blk(hl, n, m), gcs[:, n, :], f32(blk(hh, n, m)), ALU.subtract).then_inc(z_ready, 1)
                    if n == NG - 1:
                        split_next(2)

            steps = [0]

            def then(ins):
                steps[0] += 1
                ins.then_inc(ln_step, 1)
                dve.wait_ge(ln_step, steps[0])

            def tree(src, out, done):
                h = GCOLS // 2
                then(dve.tensor_tensor(lnt[:, 0:h], src[:, 0:h], src[:, h:2 * h], ALU.add))
                then(dve.tensor_tensor(lnt[:, 0:h // 2], lnt[:, 0:h // 2], lnt[:, h // 2:h], ALU.add))
                dve.tensor_tensor(out, lnt[:, 0:TG], lnt[:, TG:2 * TG], ALU.add).then_inc(done, 1)

            def over_blocks(ap):
                return ap.rearrange("p (a t) -> p a t", a=1).to_broadcast([P, KD, TG])

            def side(what, i, *rest):
                n = NORMS[i][2] if i < len(NORMS) else None
                if what == "sum":
                    name, value = rest[0]
                    dve.wait_ge(sems[name], value)
                    wait(dve, mean_full, i)
                    wait(dve, var_sum, i)
                    tree(grp(acc, n), s_mean[:], mean_sum)
                elif what == "mean":
                    dve.wait_ge(mean_full, i + 1)
                    dve.tensor_tensor(grp3(acc, n), grp3(acc, n), over_blocks(ps[:, LN_BANK, 0:TG]), ALU.subtract).then_inc(centred, 1)
                elif what == "vsum":
                    dve.wait_ge(squared, i + 1)
                    wait(dve, rstd_done, i)
                    tree(lnt[:], s_var[:], var_sum)
                elif what == "var":
                    dve.wait_ge(var_full, i + 1)
                    wait(dve, rstd_done, i)
                    dve.tensor_scalar(var[:], ps[:, LN_BANK, 0:TG], EPS, None, ALU.add).then_inc(var_copied, 1)
                elif what == "rstd":
                    dve.wait_ge(std_done, i + 1)
                    wait(dve, normed, i)
                    then(dve.reciprocal(std[:], std[:]))
                    then(dve.scalar_tensor_tensor(out=rstd[:], in0=std[:], scalar=-0.5, in1=std[:], op0=ALU.mult, op1=ALU.mult))
                    then(dve.tensor_tensor(rstd[:], rstd[:], var[:], ALU.mult))
                    dve.scalar_tensor_tensor(out=rstd[:], in0=rstd[:], scalar=1.5, in1=std[:], op0=ALU.add,
                                             op1=ALU.mult).then_inc(rstd_done, 1)
                elif what == "norm":
                    dve.wait_ge(rstd_done, i + 1)
                    dve.tensor_tensor(grp3(acc, n), grp3(acc, n), over_blocks(rstd[:]), ALU.mult).then_inc(normed, 1)
                elif what == "lo":
                    dve.wait_ge(ln_hi, mixed(i))
                    dve.tensor_tensor(grp(hl, n), grp(acc, n), f32(grp(hh, n)), ALU.subtract).then_inc(h_ready, 1)
                elif what == "centre":
                    n, q = i // 4, i % 4
                    res = sums(i)
                    dve.wait_ge(win_done, i + 1)
                    if n == 0:
                        at = V_RATIO + q * HIST
                        ratio = vec[:, at:at + HIST].rearrange("p (a t) -> p a t", a=1).to_broadcast([P, 2, HIST])
                        dve.tensor_tensor(res[:, :, HIST:2 * HIST], res[:, :, HIST:2 * HIST], ratio, ALU.mult).then_inc(d_step, 1)
                        dve.wait_ge(d_step, i + 1)
                    for a, b, off in pieces(n):
                        last = dve.scalar_tensor_tensor(out=res[:, :, a + off:b + off], in0=res[:, :, a + off:b + off],
                                                        scalar=1.0 / WINDOWS[q], in1=grp3(acc, n)[:, 2 * q:2 * q + 2, a:b],
                                                        op0=ALU.mult, op1=ALU.subtract)
                    last.then_inc(d_done, 1)
                elif what == "split":
                    n, q = i // 4, i % 4
                    dve.wait_ge(d_hi_done, i + 1)
                    for a, b, off in pieces(n):
                        last = dve.tensor_tensor(grp3(hl, n)[:, 2 * q:2 * q + 2, a:b], sums(i)[:, :, a + off:b + off],
                                                 f32(grp3(hh, n)[:, 2 * q:2 * q + 2, a:b]), ALU.subtract)
                    last.then_inc(d_ready, 1)
                elif what == "gadd":
                    n, m = i // KD, i % KD
                    if i == (NG - 1) * KD:
                        dve.wait_ge(state_out, 32)
                    dve.wait_ge(y_scaled, i + 1)
                    dve.scalar_tensor_tensor(out=blk(acc, n, m), in0=blk(acc, n, m), scalar=ALPHA, in1=gs[:, i % 2, :],
                                             op0=ALU.mult, op1=ALU.add).then_inc(y_added, 1)

            def do(step):
                if step.kind == "out":
                    n, m, i = step.n, step.m, step.a
                    dve.wait_ge(out_full, i + 1)
                    dve.scalar_tensor_tensor(out=blk(acc, n, m), in0=f32(blk(xh, n, m)), scalar=ALPHA, in1=ps[:, i % 2, 0:TG],
                                             op0=ALU.mult, op1=ALU.add).then_inc(out_free, 1)
                    dve.wait_ge(out_free, i + 1)
                    dve.scalar_tensor_tensor(out=blk(acc, n, m), in0=f32(blk(xl, n, m)), scalar=ALPHA, in1=blk(acc, n, m),
                                             op0=ALU.mult, op1=ALU.add).then_inc(out_added, 1)
                elif step.kind == "ple":
                    n, m = step.n, step.m
                    e = tt[:, step.t_buf, :]
                    dve.wait_ge(a_free, step.a + 1)
                    dve.wait_ge(b_full, step.b + 1)
                    dve.tensor_tensor(e, e, ps[:, B_BANK + step.bank, 0:TG], ALU.mult).then_inc(b_free, 1)
                    dve.wait_ge(b_free, step.b + 1)
                    dve.scalar_tensor_tensor(out=blk(acc, n, m), in0=blk(acc, n, m), scalar=ALPHA, in1=e,
                                             op0=ALU.mult, op1=ALU.add).then_inc(gate_added, 1)
                elif step.kind == "up":
                    r = (step.part, step.slot)
                    dve.wait_ge(r_hi_done, step.t + 1)
                    dve.tensor_tensor(rpart(rl, *r), tt[:, step.bank, :], f32(rpart(rh, *r)), ALU.subtract).then_inc(r_ready, 1)
                elif step.kind == "down":
                    for i, m in enumerate(step.blocks):
                        dve.wait_ge(b_full, step.b + (i + 1))
                        dve.tensor_tensor(blk(acc, step.n, m), blk(acc, step.n, m), ps[:, B_BANK + (step.bank + i) % 4, 0:TG],
                                          ALU.add).then_inc(b_free, 1)
                for u, slot, _ in step.refill:
                    split_lo(u, slot)
                for x in step.side:
                    side(*x)

            split_x(0, 0)
            split_lo(first_units[0], 0)
            split_x(0, 1)
            split_lo(first_units[1], 1)
            split_lo(first_units[2], 2)
            for n in range(1, NG):
                for h in range(2):
                    split_x(n, h)
            dve.wait_ge(small_in, 48)
            dve.wait_ge(setup, 3)
            conv_in(0)
            with dve.Fori(1, KD) as m:
                conv_in(m)
            walk(dve, plan, do)

        @block.gpsimd
        def _(pool):
            pool.memset(ub[:, 0:CH], 0.0).then_inc(setup, 1)
            pool.memset(ones[:], 1.0 / D).then_inc(setup, 1)
            pool.memset(zeros[:], 0.0).then_inc(setup, 1)
            pool.wait_ge(small_in, 48)

            def state(m):
                static = isinstance(m, int)
                hist = chist[:, m * CH:(m + 1) * CH] if static else chist[:, bass.ds(m * CH, CH)]
                wait(pool, tap2, m * 3)
                pool.sem_inc(pool_passed, 1)
                pool.tensor_copy(ub[:, CH + PROMPT:2 * CH + PROMPT], hist).then_inc(hist_in, 1)
                pool.wait_ge(u_done, m * 3 + 3)
                pool.sem_inc(pool_passed, 1)
                for part, at in enumerate((PROMPT, UW - CH)):
                    col = m * 2 * CH + part * CH
                    dst = cnew[:, col:col + CH] if static else cnew[:, bass.ds(col, CH)]
                    last = pool.tensor_copy(dst, ub[:, at:at + CH])
                last.then_inc(u_saved, 1)

            state(0)
            with pool.Fori(1, KD) as m:
                state(m)

            n_steps = [0]

            def window_sums(w):
                n, q = w // 4, w % 4
                end = WIN if n == NG - 1 else HIST + TG
                src, dst = wa[w % 2], wb[w % 2]
                pool.wait_ge(win_in, w + 1)
                wait(pool, d_ready, w - 1)
                lag, have = 1, 0
                while lag < WINDOWS[q]:
                    have += lag
                    ins = pool.tensor_tensor(dst[:, :, have:end], src[:, :, have:end], src[:, :, have - lag:end - lag], ALU.add)
                    src, dst = dst, src
                    lag *= 2
                    if lag < WINDOWS[q]:
                        n_steps[0] += 1
                        ins.then_inc(win_step, 1)
                        pool.wait_ge(win_step, n_steps[0])
                ins.then_inc(win_done, 1)

            for step in plan:
                for u, slot, _ in step.refill:
                    if u.by == "pool":
                        pool.wait_ge(w_hi, u.s + 1)
                        subtract_hi(pool, u, slot)
                for what, i, *_ in step.side:
                    if what == "fill":
                        window_sums(i)


def kernel(**inputs):
    import numpy as np
    import concourse.bacc as bacc
    from concourse.bass_utils import run_bass_kernel_spmd

    def a(name):
        return np.asarray(inputs[name])

    def blocks(w):
        k, m = w.shape
        return w.reshape(k // P, P, m // P, P).transpose(2, 1, 0, 3).reshape(m // P, P, k)

    def activations(prompt, sample):
        t = np.concatenate([prompt, sample], axis=0)
        return t.reshape(NG, TG, -1, P).transpose(3, 0, 2, 1)

    w_in, w_out = blocks(a("a_w_in")[0]), blocks(a("a_w_out")[0])
    w1 = [blocks(a("mlp_w1")[i]) for i in range(DEPTH)]
    w2 = [a("mlp_w2")[i].reshape(FF // P, P, D) for i in range(DEPTH)]
    gate = [blocks(a("ple_gate_w")[i]) for i in range(DEPTH)]
    ple = [a("ple_w")[i].reshape(KP, P, D) for i in range(DEPTH)]
    groups = a("b_w_grp")[0].reshape(2, 2, 2, P, 256).transpose(0, 3, 1, 2, 4).reshape(2, P, U)
    parts = {"in": lambda m, j: w_in[(1, 2, 0)[j] * KD + m],
             "out": lambda m: w_out[m],
             "grp": lambda j: groups[j],
             "ple": lambda i, k: ple[i][k],
             "gate": lambda i, m: gate[i][m],
             "mlp": lambda i, c, j: w1[i][c * CHUNK + j] if j < CHUNK else w2[i][c * CHUNK + j - CHUNK]}
    stream = [parts[name[0]](*name[1:]) for name in stream_rows()]
    p_t = [activations(a("p_prompt")[i][0], a("p_sample")[i][0]).transpose(1, 0, 2, 3).reshape(NG * P, KP * TG) for i in range(DEPTH)]

    def features(v):
        return v.reshape(-1, KD, P).transpose(2, 0, 1).reshape(P, -1)

    conv_w = a("a_conv_w")[0].reshape(3, KD, P).transpose(2, 1, 0).reshape(P, 3 * KD)
    ln = np.stack([a("ln1_g")[0], a("ln1_b")[0], a("ln2_g")[0], a("ln2_b")[0],
                   a("ln1_g")[1], a("ln1_b")[1], a("ln2_g")[1], a("ln2_b")[1]])
    ratio = np.array([[w / min(t + 1, w) for t in range(HIST)] for w in WINDOWS], np.float32).reshape(1, -1)
    arrays = {
        "x_t": activations(a("x_prompt")[0], a("x_sample")[0]).reshape(P, NG * GCOLS),
        "w_stream": np.concatenate(stream, axis=0),
        "p_t": np.concatenate(p_t, axis=0),
        "vectors": np.concatenate([conv_w, features(a("b_scale")[0]), features(ln), np.broadcast_to(ratio, (P, ratio.size))], axis=1),
        "conv_hist": a("state_conv")[0, 0].reshape(CH, KD, P).transpose(2, 1, 0).reshape(P, KD * CH),
        "pool_hist": a("state_pool")[0, 0].reshape(HIST, KD, P).transpose(2, 1, 0).reshape(P, KD * HIST),
    }
    outs = {"y_t": (P, NG * GCOLS), "conv_new": (P, KD * 2 * CH), "pool_new": (P, KD, 2 * HIST)}

    nc = bacc.Bacc("TRN2", target_bir_lowering=False, num_devices=1)
    args = []
    for name, v in arrays.items():
        arrays[name] = v = np.ascontiguousarray(v)
        args.append(nc.dram_tensor(name, v.shape, F32, kind="ExternalInput").ap())
    for name, shape in outs.items():
        args.append(nc.dram_tensor(name, shape, F32, kind="ExternalOutput").ap())
    bass_streaming_trunk(nc, *args)
    r = run_bass_kernel_spmd(nc, [arrays], core_ids=[0]).results[0]

    y = np.asarray(r["y_t"]).reshape(P, NG, KD, TG).transpose(1, 3, 2, 0).reshape(TOKENS, D)
    conv = np.asarray(r["conv_new"]).reshape(P, KD, 2, CH).transpose(2, 3, 1, 0).reshape(2, CH, D)
    pool = np.asarray(r["pool_new"]).reshape(P, KD, 2, HIST).transpose(2, 3, 1, 0).reshape(2, HIST, D)
    return (y[None, :PROMPT], y[None, PROMPT:], conv[None, 0:1], conv[None, 1:2], pool[None, 0:1], pool[None, 1:2])
```

```python
from contextlib import ExitStack
from dataclasses import dataclass, field, replace

import concourse.bass as bass
from concourse import mybir

F32 = mybir.dt.float32
F32R = mybir.dt.float32r
ALU = mybir.AluOpType
ACT = mybir.ActivationFunctionType

P = 128
D = 1024
KD = D // P
PROMPT, SAMPLE = 1024, 32
TOKENS = PROMPT + SAMPLE
NG = 3
TG = TOKENS // NG
TAIL = PROMPT - (NG - 1) * TG
FF = 4 * D
CHUNK = 2
NCH = FF // P // CHUNK
PLE = 256
KP = PLE // P
WINDOWS = (2, 4, 8, 16)
HIST = 15
CH = 2
DEPTH = 2
ALPHA = (2 * DEPTH) ** 0.25
EPS = 1e-5
U = 1024
GCOLS = KD * TG


AHEAD = (2, 5, 8)
BEHIND = 5
ALONE, PAIR, ALL = (0,), (1, 2), (0, 1, 2)
NORMS = [("mix", 0, 0), ("mix", 0, 1), ("mix", 0, 2),
         ("mlp", 0, 0), ("mix", 1, 0), ("mlp", 0, 1), ("mlp", 0, 2), ("mix", 1, 1), ("mix", 1, 2),
         ("mlp", 1, 0), ("mlp", 1, 1), ("mlp", 1, 2)]


@dataclass
class Unit:
    name: tuple
    row: int
    s: int
    q: int
    use: int
    by: str
    o: int
    before: object

    def later(self, i):
        before = self.before
        if before is not None:
            before = replace(before, o=i * 4 + before.o)
        return replace(self, s=i * 4 + self.s, use=i + self.use, o=i * 4 + self.o, row=i * 4 + self.row, before=before)


@dataclass
class Step:
    kind: str
    layer: int = 0
    n: int = 0
    m: int = 0
    blocks: object = None
    slot: int = 0
    slots: object = None
    mm: int = 0
    part: int = 0
    a: int = 0
    b: int = 0
    bank: int = 0
    t: int = 0
    t_buf: int = 0
    t_free: object = None
    r_used: int = 0
    r_need: int = 0
    final: bool = False
    body: object = None
    passes: int = 0
    refill: list = field(default_factory=list)
    side: list = field(default_factory=list)
    need: list = field(default_factory=list)

    def later(self, i):
        a, b = i * (NG * CHUNK), i * (NG * KD)
        step = replace(self, a=a + self.a, b=b + self.b, t=a + self.t, r_used=b + self.r_used, r_need=a + self.r_need,
                       refill=[(u.later(i), slot, [(sem, b + v) for sem, v in conds]) for u, slot, conds in self.refill],
                       need=[u.later(i) for u in self.need])
        if self.kind == "up":
            step.t_free = (self.t_free[0], a + self.t_free[1])
        return step


def stream_rows():
    names = [("in", m, j) for m in range(KD) for j in range(3)] + [("out", m) for m in range(KD)] + [("grp", 0), ("grp", 1)]
    for layer in range(DEPTH):
        names += [("ple", layer, k) for k in range(KP)] + [("gate", layer, m) for m in range(KD)]
        names += [("mlp", layer, c, j) for c in range(NCH) for j in range(4)]
    return {name: row for row, name in enumerate(names)}


def number_units(plan):
    rows = stream_rows()
    uses, split_by, last_in, holds, total = [0] * 4, {"dve": 0, "pool": 0}, {}, {}, [0]

    def unit(name, by, q):
        u = Unit(name=name, row=rows.get(name, 0), s=total[0], q=q, use=uses[q], by=by, o=split_by[by], before=last_in.get(q))
        uses[q] += 1
        split_by[by] += 1
        total[0] += 1
        last_in[q] = u
        return u

    first = [unit(("in", m, j), "dve", j) for m in range(KD) for j in range(3)][:3]
    for j in range(3):
        holds[j] = unit(("out", j), "dve", j)
    q = [3]

    def take(steps):
        for step in steps:
            step.need = [holds[slot] for slot in step.need]
            if step.kind == "loop":
                take(step.body)
                for _ in range(4 * (step.passes - 1)):
                    unit(None, "dve", q[0])
                    q[0] = (q[0] + 1) % 4
                for slot in range(4):
                    holds[slot] = holds[slot].later(step.passes - 1)
                continue
            for i, (name, slot, conds, by) in enumerate(step.refill):
                holds[slot] = unit(name, by, q[0])
                q[0] = (q[0] + 1) % 4
                step.refill[i] = (holds[slot], slot, conds)
            step.side = [x[:-1] + (holds[x[-1]],) if x[0] == "grp" else x for x in step.side]

    take(plan)
    return first


def make_plan():
    plan = []
    count = {"out": 0, "a": 0, "b": 0, "t": 0, "gate": 0, "part": 0}
    t_free, r_used, filled, held = [None, None], {}, [], {}
    base = [0]

    def at(j):
        return (base[0] + j) % 4

    def add(kind, **fields):
        plan.append(Step(kind, **fields))
        return plan[-1]

    def refill(step, name, slot, conds=(), by="dve"):
        if name is not None:
            step.refill.append((name, slot, list(conds), by))

    def inputs(layer, groups):
        for n, part in zip(groups, sorted(range(NG), key=lambda part: r_used.get(part, 0))):
            held[n] = part
            users = [step for step in plan if step.kind == "down" and step.part == part]
            last, conds = (users[-1], [("b_full", r_used[part])]) if users else (outputs_done, [("out_added", NG * KD)])
            refill(last, ("p", layer, n), ("p", part), conds)

    def quads(groups, emit, names, following, by):
        for half in range(2):
            for n in groups:
                for mm in range(4):
                    step = emit(half, n, mm)
                    if n == groups[0]:
                        step.need = [at(mm)]
                    if n == groups[-1]:
                        refill(step, names(4 + mm) if half == 0 else following[mm], at(mm), by=by(mm))

    def out_tile(half, n, mm):
        count["out"] += 1
        return add("out", n=n, m=4 * half + mm, slot=at(mm), a=count["out"] - 1)

    def gates(layer, groups, following, by):
        tiles = []

        def gate_tile(half, n, mm):
            a = count["a"]
            step = add("gate", layer=layer, n=n, m=4 * half + mm, slot=at(mm), a=a, bank=a % 2, t_free=t_free[a % 2])
            count["a"] += 1
            count["gate"] += 1
            t_free[a % 2] = ("gate_added", count["gate"])
            tiles.append(step)
            if len(tiles) >= 2:
                ple_tile(tiles[-2])
            return step

        def ple_tile(g):
            step = add("ple", n=g.n, m=g.m, part=held[g.n], t_buf=g.bank, a=g.a, b=count["b"], bank=count["b"] % 4)
            step.need = [4, 5, ("p", held[g.n])]
            count["b"] += 1
            r_used[held[g.n]] = count["b"]

        quads(groups, gate_tile, lambda m: ("gate", layer, m), following, by)
        ple_tile(tiles[-1])

    def visits(layer, todo, following, by=lambda j: "dve", loop_at=None):

        swap = len(todo) - 1 if len(todo) > 1 and len(todo[-1][1]) == 1 else None

        def names(v):
            if v == swap:
                return [("mlp", layer, todo[v][0], 2), ("mlp", layer, todo[v][0], 3)] + following[2:]
            if v + 1 == len(todo):
                return following
            new = [("mlp", layer, todo[v + 1][0], j) for j in range(4)]
            return new if v + 1 != swap else new[:2] + following[:2]

        later = []

        def splitter(v, j):
            return "dve" if todo[v][1] == ALL or v in (0, swap) else by(j)

        def ups(v, n):
            part = count["part"] % NG
            count["part"] += 1
            filled.append([part, count["t"] + CHUNK])
            for mm in range(CHUNK):
                a, t = count["a"], count["t"]
                step = add("up", n=n, part=part, mm=mm, slot=at(mm), a=a, bank=a % 2, t=t, r_used=r_used.get(part, 0), t_free=t_free[a % 2])
                count["a"], count["t"] = a + 1, t + 1
                t_free[a % 2] = ("r_ready", t + 1)
                if n == todo[v][1][0]:
                    step.need = [at(mm)]
                if n == todo[v][1][-1]:
                    new = (names(v)[mm], at(mm), (), splitter(v, mm))
                    if v > 0 and mm == CHUNK - 1:
                        later.append(new)
                    else:
                        refill(step, *new)

        def downs(v, n):
            part, ready = filled.pop(0)
            slots = [at(0), at(1)] if v == swap else [at(2), at(3)]
            for blocks in (range(0, 4), range(4, 8)):
                step = add("down", n=n, part=part, slots=slots, blocks=blocks, b=count["b"], bank=count["b"] % 4, r_need=ready)
                if n == todo[v][1][0]:
                    step.need = slots
                if later:
                    refill(step, *later.pop())
                count["b"] += len(blocks)
            r_used[part] = count["b"]
            if n == todo[v][1][-1]:
                for j in (2, 3):
                    refill(step, names(v)[j], slots[j - 2], [("b_full", count["b"])], splitter(v, j))

        ups(0, todo[0][1][0])
        v = 0
        while v < len(todo):
            begin, groups = len(plan), todo[v][1]
            for j in range(1, len(groups)):
                ups(v, groups[j])
                downs(v, groups[j - 1])
            if v + 1 < len(todo):
                ups(v + 1, todo[v + 1][1][0])
            downs(v, groups[-1])
            if v == loop_at:
                passes = 1
                while (todo[v + passes][1] == ALL and todo[v + passes + 1][0] == todo[v + passes][0] + 1
                       and todo[v + passes + 1][1][0] == 0 and len(todo[v + passes + 1][1]) > 1):
                    passes += 1
                    if v + passes + 1 >= len(todo):
                        break
                body = plan[begin:]
                del plan[begin:]
                add("loop", body=body, passes=passes)
                extra = passes - 1
                count["a"] += extra * NG * CHUNK
                count["t"] += extra * NG * CHUNK
                count["b"] += extra * NG * KD
                for n in ALL:
                    r_used[n] += extra * NG * KD
                filled[0][1] += extra * NG * CHUNK
                for x in range(2):
                    t_free[x] = (t_free[x][0], t_free[x][1] + extra * NG * CHUNK)
                v += extra
            v += 1
        if swap is not None:
            base[0] = at(2)

    def norm(i, done, lo=13):
        n = NORMS.index(i)
        rows = {0: [("sum", n, done)], 2: [("mean", n)], 3: [("square", n)], 4: [("vsum", n)], 6: [("var", n)], 7: [("rstd", n)],
                9: [("norm", n)], 10: [("affine", n, 0)], 11: [("affine", n, 1)]}
        if i[0] == "mix":
            rows.update({12: [("hi", n)], lo: [("lo", n)]})
        return rows

    def pooling(n):
        rows = {}
        for q, (fill, centre) in enumerate(((0, 2), (2, 4), (4, 6), (5, 8))):
            rows.setdefault(fill, []).append(("fill", 4 * n + q))
            rows.setdefault(centre, []).append(("centre", 4 * n + q))
            for j in range(2):
                rows.setdefault(centre + j + 3, []).append(("gadd", 8 * n + 2 * q + j))
                rows.setdefault(centre + j + 2, []).append(("grp", 8 * n + 2 * q + j, 4 + q // 2))
        return rows

    def behind(first, *chains):
        steps = [step for step in plan[first:] if step.kind not in ("ple", "refill")]
        for start, rows in chains:
            for at, parts in rows.items():
                steps[min(start + at, len(steps) - 1)].side += parts

    dve, both, first_two = (lambda j: "dve"), (lambda j: ("dve", "pool")[j % 2]), (lambda j: ("pool", "dve")[j // 2])
    gate0, gate1 = ([("gate", layer, m) for m in range(4)] for layer in range(DEPTH))
    mlp0, mlp1 = ([("mlp", layer, 0, j) for j in range(4)] for layer in range(DEPTH))

    start = add("refill")
    refill(start, ("out", 3), 3)
    conv_done = [("z_ready", KD * NG), ("u_saved", KD)]
    refill(start, ("ple", 0, 0), 4, conv_done)
    refill(start, ("ple", 0, 1), 5, conv_done)
    here = len(plan) + KD - 1
    quads(ALONE, out_tile, lambda m: ("out", m), [("out", m) for m in range(4)], dve)
    quads(PAIR, out_tile, lambda m: ("out", m), gate0, dve)
    outputs_done = add("refill")
    inputs(0, ALONE)
    gates(0, ALONE, mlp0, both)
    first, ahead = AHEAD[:2]
    visits(0, [(c, ALONE) for c in range(first)], gate0, first_two)
    inputs(0, PAIR)
    behind(here, (0, norm(("mix", 0, 0), ("out_added", 8))), (12, norm(("mix", 0, 1), ("out_added", 20), 14)),
           (18, norm(("mix", 0, 2), ("out_added", 24))))
    gates(0, PAIR, mlp0, dve)
    ple_used = [("b_full", count["b"])]
    todo = [(c, PAIR) for c in range(first)] + [(c, ALL) for c in range(first, NCH - ahead)]
    todo += [(c, ALONE) for c in range(NCH - ahead, NCH)] + [(c, PAIR) for c in range(NCH - ahead, NCH)]
    visits(0, todo, gate1, first_two, loop_at=first + 1)

    here = max(i for i, s in enumerate(plan) if s.kind == "down" and s.n == 0)
    for j in range(2):
        refill(plan[here], ("grp", j), 4 + j, ple_used)
    behind(here, (0, norm(("mlp", 0, 0), ("b_free", plan[here].b + 4))), (12, pooling(0)), (24, norm(("mix", 1, 0), ("y_added", 8))))
    done = [("b_free", s.b + 4) for n in PAIR for s in [[s for s in plan if s.kind == "down" and s.n == n][-1]]]
    step = add("refill")
    refill(step, ("ple", 1, 0), 4, [("grp_full", 8)])
    refill(step, ("ple", 1, 1), 5, [("grp_full", 8)])
    inputs(1, ALONE)
    here = max(i for i, s in enumerate(plan) if s.kind == "down" and s.n == 1)
    gates(1, ALONE, mlp1, both)
    step = add("refill")
    for j in range(2):
        refill(step, ("grp", j), 4 + j, [("b_full", count["b"])])
    ahead = AHEAD[2]
    visits(1, [(c, ALONE) for c in range(ahead)], gate1, first_two)
    step = add("refill")
    refill(step, ("ple", 1, 0), 4, [("grp_full", 24)])
    refill(step, ("ple", 1, 1), 5, [("grp_full", 24)])
    inputs(1, PAIR)
    gates(1, PAIR, mlp1, dve)
    behind(here, (0, norm(("mlp", 0, 1), done[0])), (8, norm(("mlp", 0, 2), done[1])), (12, pooling(1)), (20, pooling(2)),
           (24, norm(("mix", 1, 1), ("y_added", 16), 14)), (32, norm(("mix", 1, 2), ("y_added", 24))))
    todo = [(c, PAIR) for c in range(ahead)] + [(c, ALL) for c in range(ahead, NCH - BEHIND)]
    todo += [(c, (0, 1)) for c in range(NCH - BEHIND, NCH)] + [(c, (2,)) for c in range(NCH - BEHIND, NCH)]
    visits(1, todo, [None] * 4, first_two, loop_at=ahead + 1)
    here = max(i for i, s in enumerate(plan) if s.kind == "down" and s.n == 0)
    done = [("b_free", [s for s in plan if s.kind == "down" and s.n == n][-1].b + 4) for n in ALL]
    behind(here, (0, norm(("mlp", 1, 0), done[0])), (8, norm(("mlp", 1, 1), done[1])))
    for step in plan[-2:]:
        step.final = True
    add("rest").side.append(("finish", NORMS.index(("mlp", 1, 2))))
    return plan


def bass_streaming_trunk(nc, x_t, w_stream, p_t, vectors, conv_hist, pool_hist, y_t, conv_new, pool_new):
    plan = make_plan()
    first_units = number_units(plan)
    V_SCALE, V_LN, V_RATIO = 3 * KD, 4 * KD, 4 * KD + 4 * 2 * KD
    NV = V_RATIO + len(WINDOWS) * HIST

    with ExitStack() as ctx:
        cursor = [-(-nc.sbuf_base // 32) * 32]

        def place(name, shape, dt, at=None):
            size = 4
            for n in shape[1:]:
                size *= n
            size = -(-size // 32) * 32
            if at is None:
                at = cursor[0]
                cursor[0] += size
            return nc.alloc_sbuf_tensor_at(name, shape, dt, offset=at), at + size

        def sem(name):
            sems[name] = ctx.enter_context(nc.semaphore(name))
            return sems[name]

        sems = {}

        big = [P, NG * GCOLS]
        at1 = cursor[0]
        xh, _ = place("x_hi", big, F32R)
        acc, _ = place("acc", big, F32, at1)
        at2 = cursor[0]
        xl, end2 = place("x_lo", big, F32R)
        at3 = at2 + -(-GCOLS * 4 // 32) * 32
        WIN = HIST + TG + HIST
        w0, at = place("win_0", [P, 2, WIN], F32, at2)
        w1, at = place("win_1", [P, 2, WIN], F32, at)
        w2, at = place("win_2", [P, 2, WIN], F32, at)
        assert at <= at3
        rh, at = place("r_hi", [P, NG * CHUNK * TG], F32R, at3)
        rl, at = place("r_lo", [P, NG * CHUNK * TG], F32R, at)
        tt, at = place("t", [P, 2, TG], F32, at)
        gs, at = place("y_scaled_t", [P, 2, TG], F32, at)
        assert at <= end2
        hh, at6 = place("h_hi", big, F32R)
        hl, at7 = place("h_lo", big, F32R)
        xraw, _ = place("x_raw", big, F32, at6)
        squares, _ = place("ln_squares", big, F32, at6)
        ws, _ = place("w_split", [P, 6, 2, U], F32R)
        UW = CH + PROMPT + CH + SAMPLE
        CW = TG + CH
        ub, at = place("u", [P, UW], F32, at7 + 4 * 2 * U * 4)
        gcs, at = place("gc", [P, NG, TG], F32, at)
        cv, at = place("conv", [P, NG, CW], F32, at)
        assert at <= at7 + 6 * 2 * U * 4
        raw, _ = place("w_raw", [P, 4, U], F32)
        w3, _ = place("win_3", [P, 2, WIN], F32)
        ones, _ = place("ones", [P, P], F32)
        vec, _ = place("vec", [P, NV], F32)
        zeros, _ = place("zeros", [P, 2, HIST], F32)
        chist, _ = place("conv_history", [P, KD * CH], F32)
        phist, _ = place("pool_history", [P, KD, HIST], F32)
        cnew, _ = place("conv_state", [P, KD * 2 * CH], F32)
        tails, _ = place("tails", [P, 2, KD, HIST], F32)
        s_mean, _ = place("sum_mean", [P, TG], F32)
        s_var, at = place("sum_var", [P, TG], F32)
        std, _ = place("std", [P, TG], F32, at - -(-TG * 4 // 32) * 32)
        var, _ = place("var", [P, TG], F32)
        rstd, _ = place("rstd", [P, TG], F32)
        assert cursor[0] <= nc.sbuf_usable_end, (cursor[0], nc.sbuf_usable_end)
        wa, wb = (w0, w1), (w2, w3)
        ps = ctx.enter_context(nc.psum_tensor("ps", [P, 8, 512], F32))
        LN_BANK, B_BANK, GRP_BANK = 2, 3, 7

        x_in = [[sem(f"x_in{n}_{h}") for h in range(2)] for n in range(NG)]
        small_in = sem("small_in")
        raw_in = [sem(f"raw_in{q}") for q in range(4)]
        out_done, state_out = sem("out_done"), sem("state_out")
        w_hi = sem("w_hi")
        w_lo = {"dve": sem("w_lo_dve"), "pool": sem("w_lo_pool")}
        x_hi_done, x_ready, setup = sem("x_hi_done"), sem("x_ready"), sem("setup")
        act_passed, pool_passed = sem("act_passed"), sem("pool_passed")
        gc_full, h_full, gb_full = sem("gc_full"), sem("h_full"), sem("gb_full")
        gc_copied, u_done, tap0, tap1, tap2 = (sem(n) for n in ("gc_copied", "u_done", "tap0", "tap1", "tap2"))
        zf_done, z_hi_done, z_ready = sem("zf_done"), sem("z_hi_done"), sem("z_ready")
        hist_in, u_saved = sem("hist_in"), sem("u_saved")
        out_full, out_free, out_added = sem("out_full"), sem("out_free"), sem("out_added")
        a_full, a_free, b_full, b_free = sem("a_full"), sem("a_free"), sem("b_full"), sem("b_free")
        e_done, gate_added = sem("e_done"), sem("gate_added")
        t_squared, r_hi_done, r_ready = sem("t_squared"), sem("r_hi_done"), sem("r_ready")
        win_in, win_done, d_done, d_hi_done, d_ready = (sem(n) for n in ("win_in", "win_done", "d_done", "d_hi_done", "d_ready"))
        pool_step, d_step = sem("pool_step"), sem("d_step")
        grp_full, y_scaled, y_added, tail_saved = sem("grp_full"), sem("y_scaled"), sem("y_added"), sem("tail_saved")
        mean_sum, var_sum, mean_full, var_full = (sem(n) for n in ("mean_sum", "var_sum", "mean_full", "var_full"))
        centred, squared, var_copied, std_done, rstd_done, normed, affine, ln_hi, h_ready, ln_step = (
            sem(n) for n in ("centred", "squared", "var_copied", "std_done", "rstd_done", "normed", "affine", "ln_hi", "h_ready",
                             "ln_step"))

        last_centred, last_squared, last_normed, last_affine = (
            sem(n) for n in ("last_centred", "last_squared", "last_normed", "last_affine"))

        block = ctx.enter_context(nc.Block())

        def wait(eng, s, value):
            if not isinstance(value, int) or value > 0:
                eng.wait_ge(s, value)

        def blk(t, n, k):
            at = n * GCOLS + k * TG
            return t[:, at:at + TG] if isinstance(at, int) else t[:, bass.ds(at, TG)]

        def grp(t, n):
            return t[:, n * GCOLS:(n + 1) * GCOLS]

        def half(t, n, h):
            return t[:, n * GCOLS + h * GCOLS // 2:n * GCOLS + (h + 1) * GCOLS // 2]

        def grp3(t, n):
            return grp(t, n).rearrange("p (k t) -> p k t", k=KD)

        def f32(ap):
            return ap.bitcast(F32)

        def rpart(t, n, f):
            at = (n * CHUNK + f) * TG
            return t[:, at:at + TG]

        def vcol(at):
            return vec[:, at:at + 1]

        def pieces(n):
            return ((0, TG, HIST),) if n < NG - 1 else ((0, TAIL, HIST), (TAIL, TG, 2 * HIST))

        def sums(w):
            return (wb if w % 2 == 0 else wa)[w % 2]

        def norm_of(i):
            kind, layer, n = NORMS[i]
            return kind, layer, n, (2 * layer + (kind == "mlp")) * 2 * KD + V_LN

        def mixed(i):
            return sum(k == "mix" for k, _, _ in NORMS[:i + 1])

        def subtract_hi(eng, u, slot):
            if isinstance(slot, tuple):
                cols = slice(slot[1] * KP * TG, (slot[1] + 1) * KP * TG)
                ins = eng.tensor_tensor(rl[:, cols], raw[:, u.q, 0:KP * TG], f32(rh[:, cols]), ALU.subtract)
            else:
                ins = eng.tensor_tensor(ws[:, slot, 1, :], raw[:, u.q, :], f32(ws[:, slot, 0, :]), ALU.subtract)
            ins.then_inc(w_lo[u.by], 1)

        def walk(eng, steps, do):
            for step in steps:
                if step.kind == "loop":
                    with eng.Fori(0, step.passes) as i:
                        for inner in step.body:
                            do(inner.later(i))
                else:
                    do(step)

        @block.sync
        def _(sp):
            def load(u):
                if u.before is not None:
                    sp.wait_ge(w_lo[u.before.by], u.before.o + 1)
                if u.name is not None and u.name[0] == "p":
                    row = (u.name[1] * NG + u.name[2]) * P
                    sp.dma_start(raw[:, u.q, 0:KP * TG], p_t[row:row + P, :]).then_inc(raw_in[u.q], 16)
                else:
                    at = u.row * P
                    src = w_stream[at:at + P, :] if isinstance(at, int) else w_stream[bass.ds(at, P), :]
                    sp.dma_start(raw[:, u.q, :], src).then_inc(raw_in[u.q], 16)

            def x_load(n, h):
                sp.dma_start(half(xraw, n, h), half(x_t, n, h)).then_inc(x_in[n][h], 16)

            x_load(0, 0)
            load(first_units[0])
            x_load(0, 1)
            load(first_units[1])
            load(first_units[2])
            sp.dma_start(vec[:], vectors).then_inc(small_in, 16)
            sp.dma_start(chist[:], conv_hist).then_inc(small_in, 16)
            sp.dma_start(phist[:], pool_hist.rearrange("p (k t) -> p k t", k=KD)).then_inc(small_in, 16)
            for n in range(1, NG):
                for h in range(2):
                    x_load(n, h)
            with sp.Fori(1, KD + 1) as m:
                for j in range(3):
                    sp.wait_ge(w_lo["dve"], m * 3 + (j - 2))
                    sp.dma_start(raw[:, j, :], w_stream[bass.ds((m * 3 + j) * P, P), :]).then_inc(raw_in[j], 16)

            def do(step):
                for u, _, _ in step.refill:
                    load(u)

            walk(sp, plan, do)
            sp.wait_ge(u_saved, KD)
            sp.dma_start(conv_new, cnew[:]).then_inc(out_done, 16)
            for n in range(NG - 1):
                for h in range(2):
                    sp.wait_ge(affine, (len(NORMS) - NG + n) * 2 + h + 1)
                    sp.dma_start(half(y_t, n, h), half(acc, n, h)).then_inc(out_done, 16)
            for k in range(0, KD, 2):
                sp.wait_ge(last_affine, k + 2)
                cols = slice((NG - 1) * GCOLS + k * TG, (NG - 1) * GCOLS + (k + 2) * TG)
                sp.dma_start(y_t[:, cols], acc[:, cols]).then_inc(out_done, 16)
            sp.wait_ge(out_done, 16 * (2 * (NG - 1) + KD // 2 + 1))
            sp.wait_ge(state_out, 32)

        @block.tensor
        def _(pe):
            def triple(out, slot, col, mov_h, mov_l, first, last):
                wh, wl = ws[:, slot, 0, col:col + P], ws[:, slot, 1, col:col + P]
                pe.matmul(out, wh, mov_h, start=first, stop=False)
                pe.matmul(out, wh, mov_l, start=False, stop=False)
                return pe.matmul(out, wl, mov_h, start=False, stop=last)

            def full_tile(bank, slot, src_h, src_l, n):
                for k in range(KD):
                    mm = triple(ps[:, bank, 0:TG], slot, k * P, blk(src_h, n, k), blk(src_l, n, k), k == 0, k == KD - 1)
                return mm

            def conv_in(m):
                for n in range(NG):
                    for j, (full, freed) in enumerate(((gc_full, gc_copied), (h_full, u_done), (gb_full, zf_done))):
                        if n == 0:
                            wait(pe, w_lo["dve"], m * 3 + (j + 1))
                        wait(pe, freed, m * 3 + n)
                        for k in range(KD):
                            if isinstance(m, int) and j == 0 and k % (KD // 2) == 0:
                                pe.wait_ge(x_ready, n * 2 + k // (KD // 2) + 1)
                            mm = triple(ps[:, j, 0:TG], j, k * P, blk(xh, n, k), blk(xl, n, k), k == 0, k == KD - 1)
                        mm.then_inc(full, 1)

            def side(what, i, *rest):
                if what == "finish":
                    side("mean", i)
                    n = NORMS[i][2]
                    wait(pe, y_scaled, NG * KD)
                    for k in range(KD):
                        pe.wait_ge(last_squared, k + 1)
                        last = pe.matmul(ps[:, GRP_BANK, 0:TG], ones[:], blk(squares, n, k), start=k == 0, stop=k == KD - 1)
                    last.then_inc(var_full, 1)
                elif what == "mean":
                    pe.wait_ge(mean_sum, i + 1)
                    wait(pe, var_copied, i)
                    pe.matmul(ps[:, LN_BANK, 0:TG], ones[:], s_mean[:], start=True, stop=True).then_inc(mean_full, 1)
                elif what == "var":
                    pe.wait_ge(var_sum, i + 1)
                    pe.wait_ge(centred, i + 1)
                    pe.matmul(ps[:, LN_BANK, 0:TG], ones[:], s_var[:], start=True, stop=True).then_inc(var_full, 1)
                elif what == "grp":
                    n, m = i // KD, i % KD
                    q = m // 2
                    pe.wait_ge(w_lo[rest[0].by], rest[0].o + 1)
                    pe.wait_ge(d_ready, n * 4 + q + 1)
                    wait(pe, y_scaled, i)
                    for k in range(2):
                        col = ((q % 2) * 2 + k) * 256 + (m % 2) * P
                        last = triple(ps[:, GRP_BANK, 0:TG], 4 + q // 2, col, blk(hh, n, 2 * q + k), blk(hl, n, 2 * q + k),
                                      k == 0, k == 1)
                    last.then_inc(grp_full, 1)

            def do(step):
                for u in step.need:
                    pe.wait_ge(w_lo[u.by], u.o + 1)
                if step.kind == "out":
                    wait(pe, out_free, step.a - 1)
                    full_tile(step.a % 2, step.slot, hh, hl, step.n).then_inc(out_full, 1)
                elif step.kind == "gate":
                    if step.m == 0:
                        pe.wait_ge(h_ready, step.layer * NG + step.n + 1)
                    if step.a < 2:
                        pe.wait_ge(out_free, 24)
                    else:
                        pe.wait_ge(a_free, step.a - 1)
                    full_tile(step.bank, step.slot, hh, hl, step.n).then_inc(a_full, 1)
                elif step.kind == "ple":
                    wait(pe, b_free, step.b - 3)
                    for k in range(KP):
                        last = triple(ps[:, B_BANK + step.bank, 0:TG], 4 + k, step.m * P, rpart(rh, step.part, k), rpart(rl, step.part, k),
                                      k == 0, k == KP - 1)
                    last.then_inc(b_full, 1)
                elif step.kind == "up":
                    pe.wait_ge(a_free, step.a - 1)
                    full_tile(step.bank, step.slot, hh, hl, step.n).then_inc(a_full, 1)
                elif step.kind == "down":
                    pe.wait_ge(r_ready, step.r_need)
                    for i, m in enumerate(step.blocks):
                        pe.wait_ge(b_free, step.b + (i - 3))
                        for f in range(CHUNK):
                            last = triple(ps[:, B_BANK + (step.bank + i) % 4, 0:TG], step.slots[f], m * P, rpart(rh, step.part, f),
                                          rpart(rl, step.part, f), f == 0, f == CHUNK - 1)
                        last.then_inc(b_full, 1)
                for x in step.side:
                    side(*x)

            pe.wait_ge(setup, 3)
            conv_in(0)
            with pe.Fori(1, KD) as m:
                conv_in(m)
            pe.wait_ge(z_ready, KD * NG)
            walk(pe, plan, do)

        @block.scalar
        def _(act):
            def split_hi(u, slot, conds=()):
                act.wait_ge(raw_in[u.q], u.use * 16 + 16)
                for name, value in conds:
                    wait(act, sems[name], value)
                if isinstance(slot, tuple):
                    n = slot[1]
                    act.copy(rh[:, n * KP * TG:(n + 1) * KP * TG], raw[:, u.q, 0:KP * TG]).then_inc(w_hi, 1)
                else:
                    act.copy(ws[:, slot, 0, :], raw[:, u.q, :]).then_inc(w_hi, 1)

            def split_x(n, h):
                act.wait_ge(x_in[n][h], 16)
                act.copy(half(xh, n, h), half(xraw, n, h)).then_inc(x_hi_done, 1)

            def conv_in(m):
                def split_next(j):
                    act.wait_ge(raw_in[j], m * 16 + 32)
                    act.copy(ws[:, j, 0, :], raw[:, j, :]).then_inc(w_hi, 1)

                for n in range(NG):
                    act.wait_ge(gc_full, m * 3 + (n + 1))
                    wait(act, z_ready, m * 3 + (n - 2))
                    act.copy(gcs[:, n, :], ps[:, 0, 0:TG]).then_inc(gc_copied, 1)
                    if n == NG - 1:
                        split_next(0)
                        act.wait_ge(hist_in, m + 1)
                    act.wait_ge(u_done, m * 3 + (n + 1))
                    act.sem_inc(act_passed, 1)
                    width = TG if n < NG - 1 else CW
                    w0 = vec[:, bass.ds(m * 3, 1)] if not isinstance(m, int) else vec[:, m * 3:m * 3 + 1]
                    act.mul(cv[:, n, 0:width], ub[:, n * TG:n * TG + width], w0).then_inc(tap0, 1)
                    if n == NG - 1:
                        split_next(1)
                    act.wait_ge(zf_done, m * 3 + (n + 1))
                    act.sem_inc(act_passed, 1)
                    act.copy(blk(hh, n, m), gcs[:, n, :]).then_inc(z_hi_done, 1)
                    if n == NG - 1:
                        split_next(2)

            def side(what, i, *rest):
                if what == "finish":
                    n, at = norm_of(i)[2:]
                    for k in range(KD):
                        act.wait_ge(last_centred, k + 1)
                        act.activation(blk(squares, n, k), blk(acc, n, k), ACT.Square).then_inc(last_squared, 1)
                    side("var", i)
                    for k in range(KD):
                        act.wait_ge(last_normed, k + 1)
                        act.activation(blk(acc, n, k), blk(acc, n, k), ACT.Identity, bias=vcol(at + KD + k),
                                       scale=vcol(at + k)).then_inc(last_affine, 1)
                elif what == "square":
                    act.wait_ge(centred, i + 1)
                    act.activation(grp(squares, NORMS[i][2]), grp(acc, NORMS[i][2]), ACT.Square).then_inc(squared, 1)
                elif what == "var":
                    act.wait_ge(var_copied, i + 1)
                    wait(act, rstd_done, i)
                    act.activation(std[:], var[:], ACT.Sqrt).then_inc(std_done, 1)
                elif what == "affine":
                    kind, layer, n, at = norm_of(i)
                    h, = rest
                    act.wait_ge(normed, i + 1)
                    for k in range(4 * h, 4 * h + 4):
                        last = act.activation(blk(acc, n, k), blk(acc, n, k), ACT.Identity, bias=vcol(at + KD + k), scale=vcol(at + k))
                    last.then_inc(affine, 1)
                    if (kind, layer, h) == ("mlp", 0, 1):
                        act.wait_ge(affine, 2 * i + 2)
                        if n < NG - 1:
                            act.copy(tails[:, n, :, :], grp3(acc, n)[:, :, TG - HIST:TG]).then_inc(tail_saved, 1)
                        else:
                            a2 = grp3(acc, n)
                            act.dma_start(pool_new[:, :, 0:HIST], a2[:, :, TAIL - HIST:TAIL]).then_inc(state_out, 16)
                            act.dma_start(pool_new[:, :, HIST:2 * HIST], a2[:, :, TG - HIST:TG]).then_inc(state_out, 16)
                elif what == "hi":
                    kind, layer, n, _ = norm_of(i)
                    act.wait_ge(affine, 2 * i + 2)
                    if layer == 0:
                        act.wait_ge(out_full, (8, 20, 24)[n])
                    act.copy(grp(hh, n), grp(acc, n)).then_inc(ln_hi, 1)
                elif what == "fill":
                    n, q = i // 4, i % 4
                    ks = slice(2 * q, 2 * q + 2)
                    src, dst = grp3(acc, n)[:, ks, :], wa[i % 2]
                    act.wait_ge(affine, 2 * NORMS.index(("mlp", 0, n)) + 2)
                    wait(act, d_ready, i - 1)
                    if n == 0:
                        act.copy(dst[:, :, 0:HIST], zeros[:])
                    else:
                        act.wait_ge(tail_saved, n)
                        act.copy(dst[:, :, 0:HIST], tails[:, n - 1, ks, :])
                    if n < NG - 1:
                        act.copy(dst[:, :, HIST:HIST + TG], src).then_inc(win_in, 1)
                    else:
                        act.copy(dst[:, :, HIST:HIST + TAIL], src[:, :, 0:TAIL])
                        act.copy(dst[:, :, HIST + TAIL:2 * HIST + TAIL], phist[:, ks, :])
                        act.copy(dst[:, :, 2 * HIST + TAIL:WIN], src[:, :, TAIL:TG]).then_inc(win_in, 1)
                elif what == "grp":
                    m = i % KD
                    act.wait_ge(grp_full, i + 1)
                    wait(act, y_added, i - 1)
                    act.mul(gs[:, i % 2, :], ps[:, GRP_BANK, 0:TG], vcol(V_SCALE + m)).then_inc(y_scaled, 1)

            def do(step):
                if step.kind == "gate":
                    act.wait_ge(a_full, step.a + 1)
                    if step.t_free is not None:
                        act.wait_ge(sems[step.t_free[0]], step.t_free[1])
                    act.activation(tt[:, step.bank, :], ps[:, step.bank, 0:TG], ACT.Sigmoid).then_inc(a_free, 1)
                elif step.kind == "up":
                    t = tt[:, step.bank, :]
                    act.wait_ge(a_full, step.a + 1)
                    act.wait_ge(sems[step.t_free[0]], step.t_free[1])
                    act.activation(t, ps[:, step.bank, 0:TG], ACT.Relu).then_inc(a_free, 1)
                    act.wait_ge(a_free, step.a + 1)
                    act.activation(t, t, ACT.Square).then_inc(t_squared, 1)
                    act.wait_ge(t_squared, step.t + 1)
                    wait(act, b_full, step.r_used)
                    act.copy(rpart(rh, step.part, step.mm), t).then_inc(r_hi_done, 1)
                for u, slot, conds in step.refill:
                    if step.kind == "out":
                        act.wait_ge(out_full, step.a + 1)
                    split_hi(u, slot, conds)
                for x in step.side:
                    side(*x)

            split_x(0, 0)
            split_hi(first_units[0], 0)
            split_x(0, 1)
            split_hi(first_units[1], 1)
            split_hi(first_units[2], 2)
            for n in range(1, NG):
                for h in range(2):
                    split_x(n, h)
            act.wait_ge(setup, 3)
            act.wait_ge(small_in, 48)
            conv_in(0)
            with act.Fori(1, KD) as m:
                conv_in(m)
            walk(act, plan, do)

        @block.vector
        def _(dve):
            def split_lo(u, slot):
                if u.by == "dve":
                    dve.wait_ge(w_hi, u.s + 1)
                    subtract_hi(dve, u, slot)

            def split_x(n, h):
                dve.wait_ge(x_hi_done, n * 2 + h + 1)
                dve.tensor_tensor(half(xl, n, h), half(xraw, n, h), f32(half(xh, n, h)), ALU.subtract).then_inc(x_ready, 1)

            def conv_in(m):
                def split_next(j):
                    dve.wait_ge(w_hi, m * 3 + (4 + j))
                    dve.tensor_tensor(ws[:, j, 1, :], raw[:, j, :], f32(ws[:, j, 0, :]), ALU.subtract).then_inc(w_lo["dve"], 1)

                def w(j):
                    return vec[:, m * 3 + j:m * 3 + j + 1] if isinstance(m, int) else vec[:, bass.ds(m * 3 + j, 1)]

                for n in range(NG):
                    q1 = m * 3 + (n + 1)
                    dve.wait_ge(h_full, q1)
                    dve.wait_ge(gc_copied, q1)
                    at = CH + n * TG
                    if n < NG - 1:
                        dve.tensor_tensor(ub[:, at:at + TG], gcs[:, n, :], ps[:, 1, 0:TG], ALU.mult).then_inc(u_done, 1)
                    else:
                        wait(dve, u_saved, m)
                        dve.tensor_tensor(ub[:, at:at + TAIL], gcs[:, n, 0:TAIL], ps[:, 1, 0:TAIL], ALU.mult)
                        dve.tensor_tensor(ub[:, UW - SAMPLE:UW], gcs[:, n, TAIL:TG], ps[:, 1, TAIL:TG],
                                          ALU.mult).then_inc(u_done, 1)
                        split_next(0)
                    width = TG if n < NG - 1 else CW
                    for tap, before, done in ((1, tap0, tap1), (2, tap1, tap2)):
                        dve.wait_ge(before, q1)
                        dve.scalar_tensor_tensor(out=cv[:, n, 0:width], in0=ub[:, n * TG + tap:n * TG + tap + width], scalar=w(tap),
                                                 in1=cv[:, n, 0:width], op0=ALU.mult, op1=ALU.add).then_inc(done, 1)
                    if n == NG - 1:
                        split_next(1)
                    dve.wait_ge(tap2, q1)
                    dve.wait_ge(gb_full, q1)
                    if n < NG - 1:
                        dve.tensor_tensor(gcs[:, n, :], cv[:, n, 0:TG], ps[:, 2, 0:TG], ALU.mult).then_inc(zf_done, 1)
                    else:
                        dve.tensor_tensor(gcs[:, n, 0:TAIL], cv[:, n, 0:TAIL], ps[:, 2, 0:TAIL], ALU.mult)
                        dve.tensor_tensor(gcs[:, n, TAIL:TG], cv[:, n, TAIL + CH:CW], ps[:, 2, TAIL:TG],
                                          ALU.mult).then_inc(zf_done, 1)
                    dve.wait_ge(z_hi_done, q1)
                    dve.tensor_tensor(blk(hl, n, m), gcs[:, n, :], f32(blk(hh, n, m)), ALU.subtract).then_inc(z_ready, 1)
                    if n == NG - 1:
                        split_next(2)

            steps = [0]

            def then(ins):
                steps[0] += 1
                ins.then_inc(ln_step, 1)
                dve.wait_ge(ln_step, steps[0])

            def tree(src, tmp, out, done):
                h = GCOLS // 2
                then(dve.tensor_tensor(tmp[:, 0:h], src[:, 0:h], src[:, h:2 * h], ALU.add))
                then(dve.tensor_tensor(tmp[:, 0:h // 2], tmp[:, 0:h // 2], tmp[:, h // 2:h], ALU.add))
                dve.tensor_tensor(out, tmp[:, 0:TG], tmp[:, TG:2 * TG], ALU.add).then_inc(done, 1)

            def over_blocks(ap):
                return ap.rearrange("p (a t) -> p a t", a=1).to_broadcast([P, KD, TG])

            def side(what, i, *rest):
                n = NORMS[i][2] if i < len(NORMS) else None
                if what == "finish":
                    dve.wait_ge(mean_full, i + 1)
                    for k in range(KD):
                        dve.tensor_tensor(blk(acc, n, k), blk(acc, n, k), ps[:, LN_BANK, 0:TG], ALU.subtract).then_inc(last_centred, 1)
                    side("var", i, GRP_BANK)
                    side("rstd", i)
                    dve.wait_ge(rstd_done, i + 1)
                    for k in range(KD):
                        dve.tensor_tensor(blk(acc, n, k), blk(acc, n, k), rstd[:], ALU.mult).then_inc(last_normed, 1)
                elif what == "sum":
                    name, value = rest[0]
                    dve.wait_ge(sems[name], value)
                    wait(dve, mean_full, i)
                    tree(grp(acc, n), grp(squares, n), s_mean[:], mean_sum)
                elif what == "vsum":
                    dve.wait_ge(squared, i + 1)
                    wait(dve, rstd_done, i)
                    tree(grp(squares, n), grp(squares, n), s_var[:], var_sum)
                elif what == "mean":
                    dve.wait_ge(mean_full, i + 1)
                    dve.tensor_tensor(grp3(acc, n), grp3(acc, n), over_blocks(ps[:, LN_BANK, 0:TG]), ALU.subtract).then_inc(centred, 1)
                elif what == "var":
                    dve.wait_ge(var_full, i + 1)
                    wait(dve, rstd_done, i)
                    bank = rest[0] if rest else LN_BANK
                    dve.tensor_scalar(var[:], ps[:, bank, 0:TG], EPS, None, ALU.add).then_inc(var_copied, 1)
                elif what == "rstd":
                    dve.wait_ge(std_done, i + 1)
                    wait(dve, normed, i)
                    then(dve.reciprocal(std[:], std[:]))
                    then(dve.scalar_tensor_tensor(out=rstd[:], in0=std[:], scalar=-0.5, in1=std[:], op0=ALU.mult, op1=ALU.mult))
                    then(dve.tensor_tensor(rstd[:], rstd[:], var[:], ALU.mult))
                    dve.scalar_tensor_tensor(out=rstd[:], in0=rstd[:], scalar=1.5, in1=std[:], op0=ALU.add,
                                             op1=ALU.mult).then_inc(rstd_done, 1)
                elif what == "norm":
                    dve.wait_ge(rstd_done, i + 1)
                    dve.tensor_tensor(grp3(acc, n), grp3(acc, n), over_blocks(rstd[:]), ALU.mult).then_inc(normed, 1)
                elif what == "lo":
                    dve.wait_ge(ln_hi, mixed(i))
                    dve.tensor_tensor(grp(hl, n), grp(acc, n), f32(grp(hh, n)), ALU.subtract).then_inc(h_ready, 1)
                elif what == "centre":
                    n, q = i // 4, i % 4
                    res = sums(i)
                    dve.wait_ge(win_done, i + 1)
                    if n == 0:
                        at = V_RATIO + q * HIST
                        ratio = vec[:, at:at + HIST].rearrange("p (a t) -> p a t", a=1).to_broadcast([P, 2, HIST])
                        dve.tensor_tensor(res[:, :, HIST:2 * HIST], res[:, :, HIST:2 * HIST], ratio, ALU.mult).then_inc(d_step, 1)
                        dve.wait_ge(d_step, i + 1)
                    for a, b, off in pieces(n):
                        last = dve.scalar_tensor_tensor(out=res[:, :, a + off:b + off], in0=res[:, :, a + off:b + off],
                                                        scalar=1.0 / WINDOWS[q], in1=grp3(acc, n)[:, 2 * q:2 * q + 2, a:b],
                                                        op0=ALU.mult, op1=ALU.subtract)
                    last.then_inc(d_done, 1)
                    dve.wait_ge(d_done, i + 1)
                    for a, b, off in pieces(n):
                        last = dve.tensor_copy(grp3(hh, n)[:, 2 * q:2 * q + 2, a:b], res[:, :, a + off:b + off])
                    last.then_inc(d_hi_done, 1)
                    dve.wait_ge(d_hi_done, i + 1)
                    for a, b, off in pieces(n):
                        last = dve.tensor_tensor(grp3(hl, n)[:, 2 * q:2 * q + 2, a:b], res[:, :, a + off:b + off],
                                                 f32(grp3(hh, n)[:, 2 * q:2 * q + 2, a:b]), ALU.subtract)
                    last.then_inc(d_ready, 1)
                elif what == "gadd":
                    n, m = i // KD, i % KD
                    if i == (NG - 1) * KD:
                        dve.wait_ge(state_out, 32)
                    dve.wait_ge(y_scaled, i + 1)
                    dve.scalar_tensor_tensor(out=blk(acc, n, m), in0=blk(acc, n, m), scalar=ALPHA, in1=gs[:, i % 2, :],
                                             op0=ALU.mult, op1=ALU.add).then_inc(y_added, 1)

            def do(step):
                if step.kind == "out":
                    n, m, i = step.n, step.m, step.a
                    dve.wait_ge(out_full, i + 1)
                    dve.scalar_tensor_tensor(out=blk(acc, n, m), in0=f32(blk(xh, n, m)), scalar=ALPHA, in1=ps[:, i % 2, 0:TG],
                                             op0=ALU.mult, op1=ALU.add).then_inc(out_free, 1)
                    dve.wait_ge(out_free, i + 1)
                    dve.scalar_tensor_tensor(out=blk(acc, n, m), in0=f32(blk(xl, n, m)), scalar=ALPHA, in1=blk(acc, n, m),
                                             op0=ALU.mult, op1=ALU.add).then_inc(out_added, 1)
                elif step.kind == "ple":
                    n, m = step.n, step.m
                    e = tt[:, step.t_buf, :]
                    dve.wait_ge(a_free, step.a + 1)
                    dve.wait_ge(b_full, step.b + 1)
                    dve.tensor_tensor(e, e, ps[:, B_BANK + step.bank, 0:TG], ALU.mult).then_inc(b_free, 1)
                    dve.wait_ge(b_free, step.b + 1)
                    dve.scalar_tensor_tensor(out=blk(acc, n, m), in0=blk(acc, n, m), scalar=ALPHA, in1=e,
                                             op0=ALU.mult, op1=ALU.add).then_inc(gate_added, 1)
                elif step.kind == "up":
                    r = (step.part, step.mm)
                    dve.wait_ge(r_hi_done, step.t + 1)
                    dve.tensor_tensor(rpart(rl, *r), tt[:, step.bank, :], f32(rpart(rh, *r)), ALU.subtract).then_inc(r_ready, 1)
                elif step.kind == "down":
                    for i, m in enumerate(step.blocks):
                        dve.wait_ge(b_full, step.b + (i + 1))
                        dve.tensor_tensor(blk(acc, step.n, m), blk(acc, step.n, m), ps[:, B_BANK + (step.bank + i) % 4, 0:TG],
                                          ALU.add).then_inc(b_free, 1)
                        if step.final and m > 0:
                            dve.wait_ge(b_free, step.b + (i + 1))
                            if m == 1:
                                dve.wait_ge(mean_full, len(NORMS) - 1)
                            before = s_mean[:] if m > 1 else blk(acc, step.n, 0)
                            total = dve.tensor_tensor(s_mean[:], before, blk(acc, step.n, m), ALU.add)
                            if m < KD - 1:
                                then(total)
                            else:
                                total.then_inc(mean_sum, 1)
                for u, slot, _ in step.refill:
                    split_lo(u, slot)
                for x in step.side:
                    side(*x)

            split_x(0, 0)
            split_lo(first_units[0], 0)
            split_x(0, 1)
            split_lo(first_units[1], 1)
            split_lo(first_units[2], 2)
            for n in range(1, NG):
                for h in range(2):
                    split_x(n, h)
            dve.wait_ge(small_in, 48)
            dve.wait_ge(setup, 3)
            conv_in(0)
            with dve.Fori(1, KD) as m:
                conv_in(m)
            walk(dve, plan, do)

        @block.gpsimd
        def _(pool):
            pool.memset(ub[:, 0:CH], 0.0).then_inc(setup, 1)
            pool.memset(ones[:], 1.0 / D).then_inc(setup, 1)
            pool.memset(zeros[:], 0.0).then_inc(setup, 1)
            pool.wait_ge(small_in, 48)

            def state(m):
                static = isinstance(m, int)
                hist = chist[:, m * CH:(m + 1) * CH] if static else chist[:, bass.ds(m * CH, CH)]
                wait(pool, tap2, m * 3)
                pool.sem_inc(pool_passed, 1)
                pool.tensor_copy(ub[:, CH + PROMPT:2 * CH + PROMPT], hist).then_inc(hist_in, 1)
                pool.wait_ge(u_done, m * 3 + 3)
                pool.sem_inc(pool_passed, 1)
                for part, at in enumerate((PROMPT, UW - CH)):
                    col = m * 2 * CH + part * CH
                    dst = cnew[:, col:col + CH] if static else cnew[:, bass.ds(col, CH)]
                    last = pool.tensor_copy(dst, ub[:, at:at + CH])
                last.then_inc(u_saved, 1)

            state(0)
            with pool.Fori(1, KD) as m:
                state(m)

            n_steps = [0]

            def then(ins):
                n_steps[0] += 1
                ins.then_inc(pool_step, 1)
                pool.wait_ge(pool_step, n_steps[0])

            def window_sums(w):
                n, q = w // 4, w % 4
                end = WIN if n == NG - 1 else HIST + TG
                src, dst = wa[w % 2], wb[w % 2]
                pool.wait_ge(win_in, w + 1)
                wait(pool, d_ready, w - 1)
                lag, have = 1, 0
                while lag < WINDOWS[q]:
                    have += lag
                    ins = pool.tensor_tensor(dst[:, :, have:end], src[:, :, have:end], src[:, :, have - lag:end - lag], ALU.add)
                    src, dst = dst, src
                    lag *= 2
                    if lag < WINDOWS[q]:
                        then(ins)
                ins.then_inc(win_done, 1)

            for step in plan:
                for u, slot, _ in step.refill:
                    if u.by == "pool":
                        pool.wait_ge(w_hi, u.s + 1)
                        subtract_hi(pool, u, slot)
                for what, i, *rest in step.side:
                    if what == "fill":
                        window_sums(i)


def kernel(**inputs):
    import numpy as np
    import concourse.bacc as bacc
    from concourse.bass_utils import run_bass_kernel_spmd

    def a(name):
        return np.asarray(inputs[name])

    def blocks(w):
        k, m = w.shape
        return w.reshape(k // P, P, m // P, P).transpose(2, 1, 0, 3).reshape(m // P, P, k)

    def activations(prompt, sample):
        t = np.concatenate([prompt, sample], axis=0)
        return t.reshape(NG, TG, -1, P).transpose(3, 0, 2, 1)

    w_in, w_out = blocks(a("a_w_in")[0]), blocks(a("a_w_out")[0])
    w1 = [blocks(a("mlp_w1")[i]) for i in range(DEPTH)]
    w2 = [a("mlp_w2")[i].reshape(FF // P, P, D) for i in range(DEPTH)]
    gate = [blocks(a("ple_gate_w")[i]) for i in range(DEPTH)]
    ple = [a("ple_w")[i].reshape(KP, P, D) for i in range(DEPTH)]
    groups = a("b_w_grp")[0].reshape(2, 2, 2, P, 256).transpose(0, 3, 1, 2, 4).reshape(2, P, U)
    parts = {"in": lambda m, j: w_in[(1, 2, 0)[j] * KD + m],
             "out": lambda m: w_out[m],
             "grp": lambda j: groups[j],
             "ple": lambda i, k: ple[i][k],
             "gate": lambda i, m: gate[i][m],
             "mlp": lambda i, c, j: w1[i][c * CHUNK + j] if j < CHUNK else w2[i][c * CHUNK + j - CHUNK]}
    stream = [parts[name[0]](*name[1:]) for name in stream_rows()]
    p_t = [activations(a("p_prompt")[i][0], a("p_sample")[i][0]).transpose(1, 0, 2, 3).reshape(NG * P, KP * TG) for i in range(DEPTH)]

    def features(v):
        return v.reshape(-1, KD, P).transpose(2, 0, 1).reshape(P, -1)

    conv_w = a("a_conv_w")[0].reshape(3, KD, P).transpose(2, 1, 0).reshape(P, 3 * KD)
    ln = np.stack([a("ln1_g")[0], a("ln1_b")[0], a("ln2_g")[0], a("ln2_b")[0],
                   a("ln1_g")[1], a("ln1_b")[1], a("ln2_g")[1], a("ln2_b")[1]])
    ratio = np.array([[w / min(t + 1, w) for t in range(HIST)] for w in WINDOWS], np.float32).reshape(1, -1)
    arrays = {
        "x_t": activations(a("x_prompt")[0], a("x_sample")[0]).reshape(P, NG * GCOLS),
        "w_stream": np.concatenate(stream, axis=0),
        "p_t": np.concatenate(p_t, axis=0),
        "vectors": np.concatenate([conv_w, features(a("b_scale")[0]), features(ln), np.broadcast_to(ratio, (P, ratio.size))], axis=1),
        "conv_hist": a("state_conv")[0, 0].reshape(CH, KD, P).transpose(2, 1, 0).reshape(P, KD * CH),
        "pool_hist": a("state_pool")[0, 0].reshape(HIST, KD, P).transpose(2, 1, 0).reshape(P, KD * HIST),
    }
    outs = {"y_t": (P, NG * GCOLS), "conv_new": (P, KD * 2 * CH), "pool_new": (P, KD, 2 * HIST)}

    nc = bacc.Bacc("TRN2", target_bir_lowering=False, num_devices=1)
    args = []
    for name, v in arrays.items():
        arrays[name] = v = np.ascontiguousarray(v)
        args.append(nc.dram_tensor(name, v.shape, F32, kind="ExternalInput").ap())
    for name, shape in outs.items():
        args.append(nc.dram_tensor(name, shape, F32, kind="ExternalOutput").ap())
    bass_streaming_trunk(nc, *args)
    r = run_bass_kernel_spmd(nc, [arrays], core_ids=[0]).results[0]

    y = np.asarray(r["y_t"]).reshape(P, NG, KD, TG).transpose(1, 3, 2, 0).reshape(TOKENS, D)
    conv = np.asarray(r["conv_new"]).reshape(P, KD, 2, CH).transpose(2, 3, 1, 0).reshape(2, CH, D)
    pool = np.asarray(r["pool_new"]).reshape(P, KD, 2, HIST).transpose(2, 3, 1, 0).reshape(2, HIST, D)
    return (y[None, :PROMPT], y[None, PROMPT:], conv[None, 0:1], conv[None, 1:2], pool[None, 0:1], pool[None, 1:2])
```
